# Optimizing a Trainium2 kernel written in Bass

```python
import jax, jax.numpy as jnp
from jax import lax
import numpy as np

D_MODEL = 2048
BATCH = 1
SEQ = 256
DEPTH = 1
DEC_BATCH = 8
DEC_SEQ = 8
PAST_LEN = 2048
PAGE_SIZE = 128

N_META = 16
D_CONV = D_MODEL
CONV_W = 3
D_POOL = D_MODEL // 2
POOL_WINDOWS = (2, 4, 8, 16)
N_POOL_GROUPS = len(POOL_WINDOWS)
POOL_GROUP = D_POOL // N_POOL_GROUPS
POOL_OUT_GROUP = D_MODEL // N_POOL_GROUPS
MAX_WIN = max(POOL_WINDOWS)
D_FF = ((8 * D_MODEL // 3 + 255) // 256) * 256
D_IN = 3 * D_CONV + D_POOL + 2 * D_MODEL
SPLITS = (D_CONV, 2 * D_CONV, 3 * D_CONV, 3 * D_CONV + D_POOL, 3 * D_CONV + D_POOL + D_MODEL)
EPS = 1e-6

kernel_name = "gated_conv_pool_macaron_decoder_step"

def _rmsnorm(x, g):
    xf = x.astype(jnp.float32)
    r = lax.rsqrt(jnp.mean(xf * xf, axis=-1, keepdims=True) + EPS)
    return (xf * r).astype(x.dtype) * g

def _swiglu(x, wg, wu, wd):
    return (jax.nn.silu(x @ wg) * (x @ wu)) @ wd

def _short_conv(z, buf, w):
    L = z.shape[1]
    zp = jnp.concatenate([buf.astype(z.dtype), z], axis=1)
    y = w[0] * zp[:, 0:L]
    for k in range(1, CONV_W):
        y = y + w[k] * zp[:, k:k + L]
    return y, zp[:, -(CONV_W - 1):]

def _multiscale_pool(z, buf, pos):
    L = z.shape[1]
    P = MAX_WIN - 1
    zp = jnp.concatenate([buf.astype(z.dtype), z], axis=1)
    cs = jnp.cumsum(zp.astype(jnp.float32), axis=1)
    cs = jnp.concatenate([jnp.zeros_like(cs[:, :1]), cs], axis=1)
    outs = []
    for g, k in enumerate(POOL_WINDOWS):
        c0, c1 = g * POOL_GROUP, (g + 1) * POOL_GROUP
        s = cs[:, P + 1:P + 1 + L, c0:c1] - cs[:, P + 1 - k:P + 1 - k + L, c0:c1]
        cnt = jnp.minimum(k, pos + 1).astype(jnp.float32)[None, :, None]
        outs.append(s / cnt - z[:, :, c0:c1].astype(jnp.float32))
    pooled = jnp.stack(outs, axis=2).astype(z.dtype)
    return pooled, zp[:, -P:]

def _layer(x, conv_buf, pool_buf, pos, norm_ffn1, w1g, w1u, w1d, norm_mix, w_in, conv_w,
           w_conv_out, w_pool_group, pool_scale, w_o, norm_ffn2, w2g, w2u, w2d):
    b, L, _ = x.shape
    h = x + 0.5 * _swiglu(_rmsnorm(x, norm_ffn1), w1g, w1u, w1d)
    u = _rmsnorm(h, norm_mix)
    proj = u @ w_in
    b_gate, c_gate, v, z_pool, g_conv, g_pool = jnp.split(proj, SPLITS, axis=-1)
    conv_y, conv_state = _short_conv(c_gate * v, conv_buf, conv_w)
    y_conv = (b_gate * conv_y) @ w_conv_out
    pooled, pool_state = _multiscale_pool(z_pool, pool_buf, pos)
    y_pool = jnp.einsum('blgc,gcd->blgd', pooled, w_pool_group).reshape(b, L, D_MODEL) * pool_scale
    merged = jax.nn.sigmoid(g_conv) * y_conv + jax.nn.sigmoid(g_pool) * y_pool
    h = h + merged @ w_o
    h = h + 0.5 * _swiglu(_rmsnorm(h, norm_ffn2), w2g, w2u, w2d)
    return h, conv_state, pool_state

def setup_inputs(seed: int = 0) -> dict:
    key = jax.random.key(seed)
    ks = jax.random.split(key, 24)
    f32 = jnp.float32

    def nrm(k, shape, fan_in):
        return jax.random.normal(k, shape, f32) * (fan_in ** -0.5)

    def gain(k, shape):
        return 1.0 + 0.02 * jax.random.normal(k, shape, f32)

    return {
        "x_prompt": jax.random.normal(ks[0], (BATCH, SEQ, D_MODEL), f32),
        "x_sample": jax.random.normal(ks[1], (DEC_BATCH, DEC_SEQ, D_MODEL), f32),
        "state_conv": jax.random.normal(ks[2], (DEPTH, DEC_BATCH, CONV_W - 1, D_CONV), f32),
        "state_pool": jax.random.normal(ks[3], (DEPTH, DEC_BATCH, MAX_WIN - 1, D_POOL), f32),
        "meta_tokens": jax.random.normal(ks[4], (N_META, D_MODEL), f32),
        "norm_ffn1": gain(ks[5], (DEPTH, D_MODEL)),
        "w_ffn1_gate": nrm(ks[6], (DEPTH, D_MODEL, D_FF), D_MODEL),
        "w_ffn1_up": nrm(ks[7], (DEPTH, D_MODEL, D_FF), D_MODEL),
        "w_ffn1_down": nrm(ks[8], (DEPTH, D_FF, D_MODEL), D_FF),
        "norm_mix": gain(ks[9], (DEPTH, D_MODEL)),
        "w_in": nrm(ks[10], (DEPTH, D_MODEL, D_IN), D_MODEL),
        "conv_w": nrm(ks[11], (DEPTH, CONV_W, D_CONV), CONV_W),
        "w_conv_out": nrm(ks[12], (DEPTH, D_CONV, D_MODEL), D_CONV),
        "w_pool_group": nrm(ks[13], (DEPTH, N_POOL_GROUPS, POOL_GROUP, POOL_OUT_GROUP), POOL_GROUP),
        "pool_scale": gain(ks[14], (DEPTH, D_MODEL)),
        "w_o": nrm(ks[15], (DEPTH, D_MODEL, D_MODEL), D_MODEL),
        "norm_ffn2": gain(ks[16], (DEPTH, D_MODEL)),
        "w_ffn2_gate": nrm(ks[17], (DEPTH, D_MODEL, D_FF), D_MODEL),
        "w_ffn2_up": nrm(ks[18], (DEPTH, D_MODEL, D_FF), D_MODEL),
        "w_ffn2_down": nrm(ks[19], (DEPTH, D_FF, D_MODEL), D_FF),
        "norm_final": gain(ks[20], (D_MODEL,)),
    }

def reference(x_prompt, x_sample, state_conv, state_pool, meta_tokens, norm_ffn1, w_ffn1_gate,
              w_ffn1_up, w_ffn1_down, norm_mix, w_in, conv_w, w_conv_out, w_pool_group,
              pool_scale, w_o, norm_ffn2, w_ffn2_gate, w_ffn2_up, w_ffn2_down, norm_final):
    meta = jnp.broadcast_to(meta_tokens.astype(x_prompt.dtype)[None], (BATCH, N_META, D_MODEL))
    hp = jnp.concatenate([meta, x_prompt], axis=1)
    pos_p = jnp.arange(N_META + SEQ, dtype=jnp.int32)
    pos_s = PAST_LEN + jnp.arange(DEC_SEQ, dtype=jnp.int32)
    hs = x_sample
    conv_p, pool_p, conv_s, pool_s = [], [], [], []
    for l in range(DEPTH):
        lw = (norm_ffn1[l], w_ffn1_gate[l], w_ffn1_up[l], w_ffn1_down[l], norm_mix[l], w_in[l],
              conv_w[l], w_conv_out[l], w_pool_group[l], pool_scale[l], w_o[l], norm_ffn2[l],
              w_ffn2_gate[l], w_ffn2_up[l], w_ffn2_down[l])
        zbuf_c = jnp.zeros((BATCH, CONV_W - 1, D_CONV), hp.dtype)
        zbuf_p = jnp.zeros((BATCH, MAX_WIN - 1, D_POOL), hp.dtype)
        hp, cp, pp = _layer(hp, zbuf_c, zbuf_p, pos_p, *lw)
        hs, cs_, ps_ = _layer(hs, state_conv[l], state_pool[l], pos_s, *lw)
        conv_p.append(cp)
        pool_p.append(pp)
        conv_s.append(cs_)
        pool_s.append(ps_)
    y_prompt = _rmsnorm(hp[:, N_META:], norm_final)
    y_sample = _rmsnorm(hs, norm_final)
    new_conv_prompt = jnp.stack(conv_p, axis=0)
    new_pool_prompt = jnp.stack(pool_p, axis=0)
    new_conv_sample = jnp.stack(conv_s, axis=0)
    new_pool_sample = jnp.stack(pool_s, axis=0)
    return (y_prompt, y_sample, new_conv_prompt, new_pool_prompt, new_conv_sample, new_pool_sample)


_drawn_inputs = setup_inputs


def setup_inputs(seed=0):
    import zlib

    import numpy as np

    out = dict(_drawn_inputs(seed))
    spreads = {}
    factors = {'norm_ffn1': 4.47,
     'pool_scale': 33.435,
     'norm_ffn2': 8.0,
     'norm_final': 23.596,
     'state_conv': 3.967}
    for name, (base, spread) in spreads.items():
        noise = np.random.default_rng([zlib.crc32(name.encode()), seed]).standard_normal(out[name].shape)
        drawn = base * np.exp(spread * noise) if base else spread * noise
        out[name] = __import__('jax').numpy.asarray(drawn.astype(out[name].dtype))
    for name, factor in factors.items():
        out[name] = (out[name] * factor).astype(out[name].dtype)
    return out
```

```python
from contextlib import ExitStack

import concourse.bass as bass
from concourse import mybir

F32 = mybir.dt.float32
F32R = mybir.dt.float32r
ALU = mybir.AluOpType
ACT = mybir.ActivationFunctionType

P = 128
D = 2048
F = 5632
KD = D // P
META, SEQ = 16, 256
SEQS, STEPS = 8, 8
SAMP = SEQS * STEPS
T = META + SEQ + SAMP
LIVE = SEQ + SAMP
CONV_PAST = 2
CV = CONV_PAST + LIVE
POOL_PAST = 15
WINDOWS = (2, 4, 8, 16)
EPS = 1e-6

CHUNK = 1024
RAW = 8
SLOTS = 4
HELD_BACK = 5
PROJ = 4
SPREAD = 8

FFN_TURNS = F // 512
FFN_CHUNKS = 4 * PROJ + SPREAD
CONV_TURNS = D // 512
CONV_CHUNKS = 6 * PROJ + SPREAD
MIX_TURNS = D // 512
MIX_CHUNKS = 4 * PROJ + SPREAD
POOL_ORDER = (3, 2, 1, 0)
POOL_CHUNKS = 4 * (PROJ + 1)

N_FFN1 = 0
N_POOL = N_FFN1 + FFN_TURNS * FFN_CHUNKS
N_CONV = N_POOL + POOL_CHUNKS
N_MIX = N_CONV + CONV_TURNS * CONV_CHUNKS
N_FFN2 = N_MIX + MIX_TURNS * MIX_CHUNKS
N_ALL = N_FFN2 + FFN_TURNS * FFN_CHUNKS

B0, C0, V0, Z0, GC0, GP0 = 0, D, 2 * D, 3 * D, 3 * D + D // 2, 4 * D + D // 2

G_FFN1, G_MIX, G_FFN2, G_FINAL, G_SCALE, G_CONV = 0, 16, 32, 48, 64, 80

SEG_C = CONV_PAST + STEPS
PBUF = CONV_PAST + SEQ + SEQS * SEG_C
SEG_Z = POOL_PAST + STEPS
ZBUF = META + SEQ + SEQS * SEG_Z
CTAIL = CONV_PAST + SEQS * CONV_PAST
ZTAIL = POOL_PAST + SAMP

SPREAD_MIX = KD * FFN_TURNS + KD + KD * CONV_TURNS
SPREAD_FFN2 = SPREAD_MIX + KD * MIX_TURNS

POOL_PLAN = [(c, a) for a in (0, 1) for c in range(PROJ)] + [("map", 0)]
POOL_PLAN += [(c, a) for a in (2, 3) for c in range(PROJ)] + [("map", a) for a in (1, 2, 3)]
TAIL_BANKS = (2, 3, 5, 6, 7, 4)
Z_BANKS = ((4, 5), (6, 7), (4, 5), (6, 7))
MAP_BANKS = ((0, 1, 2, 3), (0, 1, 2, 3), (4, 5, 6, 7), (0, 1, 2, 3))
POOL_SPLITS = {4: 0, 8: 1, 13: 2, 17: 3}


def pool_source(a):
    return (POOL_ORDER[a] + 1) % 2


def first_of(norm):
    return META if norm >= 2 else 0


class Tally:

    def __init__(self, sem, start=0):
        self.sem, self.n, self.turns, self.per, self.first = sem, start, None, 0, 0

    def up(self, k=1):
        self.n += k

    def at(self, k=0):
        return self.n + k if self.turns is None else self.turns + (self.n + k)

    def enter(self, i, per):
        self.per, self.turns, self.first = per, i * per if per else None, self.n

    def leave(self, times):
        assert self.n - self.first == self.per, (self.sem, self.n - self.first, self.per)
        self.n, self.turns = self.first + times * self.per, None


class Chunks:

    def __init__(self):
        self.i, self.chunks = None, 0

    def enter(self, i, chunks):
        self.i, self.chunks = i, chunks

    def leave(self):
        self.i = None

    def count(self, x):
        return x if self.i is None else self.i * self.chunks + x

    def loaded(self, n):
        x = 16 * (n // RAW + 1)
        return x if self.i is None else self.i * (16 * self.chunks // RAW) + x


def build(nc, x_prompt, x_sample, state_conv, state_pool, meta_tokens, norm_ffn1, w_ffn1_gate,
          w_ffn1_up, w_ffn1_down, norm_mix, w_in, conv_w, w_conv_out, w_pool_group, pool_scale,
          w_o, norm_ffn2, w_ffn2_gate, w_ffn2_up, w_ffn2_down, norm_final,
          y_prompt, y_sample, new_conv_prompt, new_pool_prompt, new_conv_sample, new_pool_sample):
    with ExitStack() as ctx:
        def sb(name, shape, dt=F32):
            return ctx.enter_context(nc.sbuf_tensor(name, shape, dt))

        def sem(name):
            return ctx.enter_context(nc.semaphore(name))

        h = sb("h", [P, KD, T])
        xn_hi = sb("xn_hi", [P, KD, T], F32R)
        xn_lo = sb("xn_lo", [P, KD, T], F32R)
        hid_hi = sb("hid_hi", [P, 4, T], F32R)
        hid_lo = sb("hid_lo", [P, 4, T], F32R)
        raw = sb("raw", [P, RAW, CHUNK])
        w_hi = sb("w_hi", [P, SLOTS, CHUNK], F32R)
        w_lo = sb("w_lo", [P, SLOTS, CHUNK], F32R)
        acc = sb("acc", [P, 2, KD, LIVE])
        ta = sb("ta", [P, 4, T])
        tb = sb("tb", [P, 4, T])
        pbuf = sb("pbuf", [P, 4, PBUF])
        ssum = sb("ssum", [P, T])
        rstd = sb("rstd", [P, T])
        tok = sb("tok", [P, 5, 3])
        warm = sb("warm", [P, 4])
        vecs_in = sb("vecs_in", [P, P])
        vecs = sb("vecs", [P, P])
        conv_past = sb("conv_past", [P, KD, SEQS * CONV_PAST])
        pool_past = sb("pool_past", [P, KD // 2, SEQS * POOL_PAST])
        ctail = sb("ctail", [P, KD, CTAIL])
        ztail = sb("ztail", [P, KD // 2, ZTAIL])
        ident = sb("ident", [P, P])
        ones = sb("ones", [P, P])
        bank = [ctx.enter_context(nc.psum_tensor(f"bank{b}", [P, 512], F32)) for b in range(8)]

        yconv, ypool = acc[:, 0], acc[:, 1]
        acc_flat = acc[:].rearrange("p a k t -> p (a k t)")
        rows = acc_flat[:, 0:3 * D].rearrange("p (t d) -> p t d", t=3)
        squares_out = acc_flat[:, 3 * D:4 * D]
        conv_rows = acc_flat[0:SEQS * CONV_PAST, 3 * D:4 * D]
        pool_rows = acc_flat[0:SEQS * POOL_PAST, 4 * D:4 * D + D // 2]
        ctail_rows = acc_flat[0:CTAIL, 0:D]
        ztail_rows = acc_flat[0:ZTAIL, D:D + D // 2]
        flat_p = pbuf[:].rearrange("p a c -> p (a c)")
        zbuf = flat_p[:, 0:2 * ZBUF].rearrange("p (a c) -> p a c", a=2)
        rs = flat_p[:, 0:3 * T].rearrange("p (a c) -> p a c", a=3)
        sums = [x[:].rearrange("p a c -> p (a c)")[:, 0:2 * ZBUF].rearrange("p (a c) -> p a c", a=2)
                for x in (ta, tb)]
        X_ROWS = ((0, P), (P, P), (2 * P, T - 2 * P))
        Y_ROWS = ((META, P), (META + P, P), (META + SEQ, SAMP))

        def steps_of(row, seg, past):
            return row.rearrange("p (s c) -> p s c", c=seg)[:, :, past:seg]

        def past_of(row, seg, past):
            return row.rearrange("p (s c) -> p s c", c=seg)[:, :, 0:past]

        x_in = [sem(f"x_in{t}") for t in range(3)]
        vecs_in_done, states_in = sem("vecs_in_done"), sem("states_in")
        tok_set = sem("tok_set")
        loaded = [sem(f"loaded{s}") for s in range(RAW)]
        hi_done = sem("hi_done")
        lo_done = sem("lo_done")
        used = sem("used")
        ident_zero, ident_done, ones_done = sem("ident_zero"), sem("ident_done"), sem("ones_done")
        yconv_zero = sem("yconv_zero")
        turned = sem("turned")
        summed = sem("summed")
        x_copied = sem("x_copied")
        vecs_done = sem("vecs_done")
        past_done = sem("past_done")
        tok_sq = sem("tok_sq")
        diag_done = sem("diag_done")
        rstd_in = sem("rstd_in")
        sq_done = sem("sq_done")
        ssum_done = sem("ssum_done")
        root_in, root_done = sem("root_in"), sem("root_done")
        xt_done = sem("xt_done")
        xt_hi = sem("xt_hi")
        xn_done = sem("xn_done")
        gate_done = sem("gate_done")
        sig_done = sem("sig_done")
        v_done = sem("v_done")
        placed = sem("placed")
        z_done = sem("z_done")
        z_kept = sem("z_kept")
        tails_done = sem("tails_done")
        step = sem("step")
        p_done = sem("p_done")
        hid_done = sem("hid_done")
        hid_hi_done = sem("hid_hi_done")
        hid_lo_done = sem("hid_lo_done")
        spread_done = sem("spread_done")
        tail_rows = sem("tail_rows")
        hg_done = sem("hg_done")
        rows_act, rows_dve = sem("rows_act"), sem("rows_dve")
        rstd_tok = sem("rstd_tok")
        bank_full = sem("bank_full")
        tails_stored, y_stored = sem("tails_stored"), sem("y_stored")
        slot_seen_free = sem("slot_seen_free")

        def proj_view(w, c, col):
            return w.rearrange("(k p) n -> p k n", p=P)[:, 4 * c:4 * c + 4, bass.ds(col, 256)]

        def spread_view(w, k, q):
            return w.rearrange("(k p) n -> p k n", p=P)[:, bass.ds(k, 2), 512 * q:512 * q + 512]

        block = ctx.enter_context(nc.Block())

        @block.sync
        def _(sp):
            ch = Chunks()
            sp.dma_start(rows[0:META, 0, :], meta_tokens).then_inc(x_in[0], 16)
            sp.dma_start(rows[META:P, 0, :], x_prompt[0, 0:P - META, :]).then_inc(x_in[0], 16)
            sp.dma_start(rows[:, 1, :], x_prompt[0, P - META:2 * P - META, :]).then_inc(x_in[1], 16)
            sp.dma_start(rows[0:META, 2, :], x_prompt[0, 2 * P - META:SEQ, :]).then_inc(x_in[2], 16)
            sp.dma_start(rows[META:META + SAMP, 2, :],
                         x_sample.rearrange("b s d -> (b s) d")).then_inc(x_in[2], 16)
            flat = "l d -> (l d)"
            for v, (src, n) in enumerate((
                    (norm_ffn1.rearrange(flat), 16), (norm_mix.rearrange(flat), 16),
                    (norm_ffn2.rearrange(flat), 16), (norm_final, 16),
                    (pool_scale.rearrange(flat), 16), (conv_w.rearrange("l w d -> (l w d)"), 48))):
                sp.dma_start(vecs_in[16 * v:16 * v + n, :],
                             src.rearrange("(k p) -> k p", p=P)).then_inc(vecs_in_done, 16)

            def load(n, src, k_tiles, at_start=False):
                sp.wait_ge(lo_done, ch.count(n + 1))
                if at_start:
                    sp.sem_inc(slot_seen_free, 1)
                sp.dma_start(raw[:, n % RAW, :].rearrange("p (k n) -> p k n", k=k_tiles),
                             src).then_inc(loaded[n % RAW], 16)

            def blocks(n0, times, chunks, projections, spread_over):
                assert chunks % RAW == 0
                with sp.Fori(0, times) as i:
                    ch.enter(i, chunks)
                    col, k = sp.snap(i * 512), sp.snap(i * 4)
                    n = n0
                    for w, first in projections:
                        for c in range(PROJ):
                            load(n, proj_view(w, c, col + first), 4, first + c == 0)
                            n += 1
                    for q in range(4):
                        for half in range(2):
                            load(n, spread_view(spread_over, k + 2 * half, q), 2)
                            n += 1
                ch.leave()

            def ffn(n0, gate, up, down):
                blocks(n0, FFN_TURNS, FFN_CHUNKS, ((gate, 0), (up, 0), (gate, 256), (up, 256)), down)

            win = w_in[0]
            ffn(N_FFN1, w_ffn1_gate[0], w_ffn1_up[0], w_ffn1_down[0])
            for j, (kind, a) in enumerate(POOL_PLAN):
                g = POOL_ORDER[a]
                if kind == "map":
                    load(N_POOL + j, w_pool_group[0, g].rearrange("(k p) n -> p k n", p=P), 2)
                else:
                    load(N_POOL + j, proj_view(win, kind, Z0 + 256 * g), 4)
            blocks(N_CONV, CONV_TURNS, CONV_CHUNKS,
                   [(win, col) for col in (V0, C0, V0 + 256, C0 + 256, B0, B0 + 256)], w_conv_out[0])
            blocks(N_MIX, MIX_TURNS, MIX_CHUNKS,
                   [(win, col) for col in (GC0, GC0 + 256, GP0, GP0 + 256)], w_o[0])
            ffn(N_FFN2, w_ffn2_gate[0], w_ffn2_up[0], w_ffn2_down[0])

            for j in range(12):
                kg, t = j // 3, j % 3
                sp.wait_ge(rows_dve if j % 2 else rows_act, j // 2 + 1)
                dst = y_prompt[0, t * P:(t + 1) * P, :] if t < 2 else y_sample.rearrange("b s d -> (b s) d")
                sp.dma_start(dst[:, 512 * kg:512 * kg + 512],
                             rows[0:Y_ROWS[t][1], t, 512 * kg:512 * kg + 512]).then_inc(y_stored, 16)
            sp.wait_ge(y_stored, 16 * 12)

        @block.gpsimd
        def _(pool):
            pool.memset(ident[:], 0.0).then_inc(ident_zero, 1)
            pool.wait_ge(ident_zero, 1)
            pool.affine_select(out=ident[:], in_=ident[:], compare_op=ALU.not_equal, fill=1.0, base=0,
                               pattern=[[-1, P]], channel_multiplier=1).then_inc(ident_done, 1)
            pool.memset(ones[:], 1.0).then_inc(ones_done, 1)
            pool.wait_ge(tok_sq, 3)
            pool.wait_ge(x_copied, 12)
            pool.dma_start(conv_rows, state_conv.rearrange("l b w d -> (l b w) d")).then_inc(states_in, 16)
            pool.dma_start(pool_rows, state_pool.rearrange("l b w d -> (l b w) d")).then_inc(states_in, 16)
            pool.memset(yconv, 0.0).then_inc(yconv_zero, 1)
            pool.dma_start(new_pool_sample[0, :, 0:POOL_PAST - STEPS, :],
                           state_pool[0, :, STEPS:POOL_PAST, :]).then_inc(tails_stored, 16)
            pool.wait_ge(tail_rows, 6)
            pool.dma_start(new_conv_prompt[0, 0], ctail_rows[0:CONV_PAST, :]).then_inc(tails_stored, 16)
            pool.dma_start(new_conv_sample[0].rearrange("b w d -> (b w) d"),
                           ctail_rows[CONV_PAST:CTAIL, :]).then_inc(tails_stored, 16)
            pool.dma_start(new_pool_prompt[0, 0], ztail_rows[0:POOL_PAST, :]).then_inc(tails_stored, 16)
            for s in range(SEQS):
                r = POOL_PAST + STEPS * s
                pool.dma_start(new_pool_sample[0, s, POOL_PAST - STEPS:POOL_PAST, :],
                               ztail_rows[r:r + STEPS, :]).then_inc(tails_stored, 16)

        @block.tensor
        def _(pe):
            ch = Chunks()
            hid, spr, p = Tally(hid_lo_done), Tally(spread_done, KD), Tally(p_done)
            LOW, HIGH = (0, 1, 2, 3), (4, 5, 6, 7)

            def three_passes(out, slot, cols, x_hi, x_lo, start, stop):
                pe.matmul(out, w_hi[:, slot, cols], x_hi, start=start, stop=False)
                pe.matmul(out, w_hi[:, slot, cols], x_lo, start=False, stop=False)
                return pe.matmul(out, w_lo[:, slot, cols], x_hi, start=False, stop=stop)

            def project(n, banks, first_token, norm=None, between=None):
                for c in range(PROJ):
                    if between is not None and c == between[0]:
                        between[1]()
                    pe.wait_ge(lo_done, ch.count(RAW + n + c + 1))
                    for kk in range(4):
                        k = 4 * c + kk
                        if norm is not None:
                            pe.wait_ge(xn_done, KD * norm + k + 1)
                        for t, b in enumerate(banks):
                            col = kk * 256 + t * P
                            last = three_passes(bank[b][:, 0:T - first_token], (n + c) % SLOTS,
                                                slice(col, col + P), xn_hi[:, k, first_token:T],
                                                xn_lo[:, k, first_token:T], k == 0, k == KD - 1)
                    last.then_inc(used, 1)

            def spread(n, banks, width, tiles, ready=False):
                for half in range(len(tiles) // 2):
                    if ready:
                        pe.wait_ge(hid_lo_done, hid.at(2))
                        hid.up(2)
                    pe.wait_ge(lo_done, ch.count(RAW + n + half + 1))
                    for m, b in enumerate(banks):
                        for kk in range(2):
                            k = tiles[2 * half + kk]
                            col = kk * 512 + m * P
                            last = three_passes(bank[b][:, 0:width], (n + half) % SLOTS, slice(col, col + P),
                                                hid_hi[:, k, 0:width], hid_lo[:, k, 0:width],
                                                k == tiles[0], k == tiles[-1])
                        if m < 3 and k == tiles[-1]:
                            last.then_inc(bank_full, 1)
                    last.then_inc(used, 1)

            def spread_all(n, order, width):
                for q in range(4):
                    if q >= 2:
                        pe.wait_ge(spread_done, spr.at(4 * (q - 1)))
                    spread(n + 2 * q, order[q % 2], width, (0, 1, 2, 3), ready=q == 0)
                spr.up(KD)

            def loop(times, chunks, cmul, body):
                with pe.Fori(0, times) as i:
                    ch.enter(i, chunks)
                    hid.enter(i, 4)
                    spr.enter(i, KD)
                    p.enter(i, cmul)
                    body()
                ch.leave()
                for x in (hid, spr, p):
                    x.leave(times)

            def sum_squares(norm, b):
                pe.wait_ge(ssum_done, KD * norm)
                pe.matmul(bank[b][:, 0:T - first_of(norm)], ones[:], ssum[:, first_of(norm):T],
                          start=True, stop=True).then_inc(summed, 1)

            pe.wait_ge(ident_done, 1)
            for t, (first, count) in enumerate(X_ROWS):
                pe.wait_ge(x_in[t], 16 if t == 1 else 32)
                for kg in range(4):
                    if t == 2:
                        pe.wait_ge(x_copied, kg + 1)
                    for k in range(4):
                        last = pe.transpose(bank[(4 * t + kg) % 8][:, k * count:(k + 1) * count],
                                            rows[0:count, t, (4 * kg + k) * P:(4 * kg + k + 1) * P],
                                            ident[0:count, 0:count])
                    last.then_inc(turned, 1)
            pe.wait_ge(vecs_in_done, 16 * 6)
            pe.wait_ge(x_copied, 5)
            pe.transpose(bank[4][:, 0:P], vecs_in[:], ident[:]).then_inc(turned, 1)

            def spread_rstd():
                pe.wait_ge(ones_done, 1)
                pe.wait_ge(diag_done, 3)
                for t, (first, count) in enumerate(X_ROWS):
                    last = pe.matmul(bank[5][:, first:first + count], ones[0:count, :], tb[0:count, t, 0:count],
                                     start=True, stop=True)
                last.then_inc(rstd_in, 1)

            pe.sem_inc(used, SLOTS)
            pe.wait_ge(x_copied, 12)

            def ffn_block(n, first_token, norm=None, between=None):
                pe.wait_ge(spread_done, spr.at(-4))
                project(n, (0, 1), first_token, norm, between)
                if norm == 2:
                    pe.wait_ge(tail_rows, 6)
                project(n + PROJ, (2, 3), first_token)
                pe.wait_ge(spread_done, spr.at())
                project(n + 2 * PROJ, (4, 5), first_token)
                project(n + 3 * PROJ, (6, 7), first_token)
                spread_all(n + 4 * PROJ, (LOW, HIGH), T - first_token)

            def ffn(n0, first_token, norm, between):
                ffn_block(n0, first_token, norm, between)
                loop(FFN_TURNS - 1, FFN_CHUNKS, 0, lambda: ffn_block(n0 + FFN_CHUNKS, first_token))

            ffn(N_FFN1, 0, 0, (1, spread_rstd))

            pe.wait_ge(states_in, 32)
            pe.wait_ge(spread_done, spr.at(-4))
            for k in range(KD):
                last = pe.transpose(bank[1][:, 16 * k:16 * k + 16], conv_rows[:, k * P:(k + 1) * P],
                                    ident[0:16, 0:16])
            last.then_inc(turned, 1)
            for g in range(2):
                for k in range(4):
                    col = (4 * g + k) * P
                    last = pe.transpose(bank[2 + g][:, 120 * k:120 * k + 120], pool_rows[:, col:col + P],
                                        ident[0:120, 0:120])
                last.then_inc(turned, 1)
            sum_squares(1, 0)

            for j, (kind, a) in enumerate(POOL_PLAN):
                if kind == 0:
                    if a >= 2:
                        pe.wait_ge(z_kept, a - 1)
                    project(N_POOL + j, Z_BANKS[a], 0, 1)
                elif kind == "map":
                    pe.wait_ge(past_done, 3)
                    if a >= 2:
                        pe.wait_ge(z_kept, 4)
                    pe.wait_ge(spread_done, spr.at(-4 if a >= 2 else 0))
                    spread(N_POOL + j, MAP_BANKS[a], LIVE, (2 * (a % 2), 2 * (a % 2) + 1), ready=True)
                    spr.up(4)

            def conv_body():
                n = N_CONV
                pe.wait_ge(spread_done, spr.at(-2))
                project(n, (0, 1), META - CONV_PAST)
                pe.wait_ge(spread_done, spr.at())
                project(n + PROJ, (2, 3), META - CONV_PAST)
                project(n + 2 * PROJ, (4, 5), META - CONV_PAST)
                project(n + 3 * PROJ, (6, 7), META - CONV_PAST)
                pe.wait_ge(p_done, p.at(2))
                project(n + 4 * PROJ, (0, 1), META)
                project(n + 5 * PROJ, (2, 3), META)
                pe.wait_ge(p_done, p.at(4))
                p.up(4)
                spread_all(n + 6 * PROJ, (HIGH, LOW), LIVE)
            loop(CONV_TURNS, CONV_CHUNKS, 4, conv_body)

            pe.wait_ge(spread_done, spr.at(-2))

            def mix_body():
                n = N_MIX
                pe.wait_ge(spread_done, spr.at(-4))
                project(n, (0, 1), META)
                pe.wait_ge(spread_done, spr.at())
                project(n + PROJ, (2, 3), META)
                project(n + 2 * PROJ, (4, 5), META)
                project(n + 3 * PROJ, (6, 7), META)
                spread_all(n + 4 * PROJ, (LOW, HIGH), LIVE)
            loop(MIX_TURNS, MIX_CHUNKS, 0, mix_body)

            def sum_and_tails():
                sum_squares(2, 4)
                pe.wait_ge(tails_done, KD)
                for g in range(2):
                    for k in range(4):
                        last = pe.transpose(bank[2 + g][0:ZTAIL, k * P:(k + 1) * P], ztail[:, 4 * g + k, :], ident[:])
                    last.then_inc(turned, 1)
                for g in range(4):
                    if g == 3:
                        pe.wait_ge(root_in, 3)
                    for k in range(4):
                        last = pe.transpose(bank[TAIL_BANKS[2 + g]][0:CTAIL, k * P:(k + 1) * P],
                                            ctail[:, 4 * g + k, :], ident[:])
                    last.then_inc(turned, 1)

            ffn(N_FFN2, META, 2, (2, sum_and_tails))

            for j in range(12):
                kg, (first, count) = j // 3, Y_ROWS[j % 3]
                if j % 3 == 0:
                    pe.wait_ge(hg_done, 4 * kg + 4)
                if j == 0:
                    pe.wait_ge(spread_done, spr.at(-4))
                if j == 4:
                    pe.wait_ge(spread_done, spr.at())
                if j == 7:
                    pe.wait_ge(ssum_done, KD * 3)
                    for t, (at, n) in enumerate(Y_ROWS):
                        last = pe.matmul(bank[7][0:n, 2 * t:2 * t + 2], ssum[:, at:at + n], ones[:, 0:2],
                                         start=True, stop=True)
                    last.then_inc(summed, 1)
                if j >= 7:
                    pe.wait_ge(rows_act if j % 2 else rows_dve, (j - 7) // 2 + 1)
                for k in range(4):
                    last = pe.transpose(bank[j % 7][0:count, k * P:(k + 1) * P],
                                        h[:, 4 * kg + k, first:first + count], ident[:])
                last.then_inc(turned, 1)

        @block.scalar
        def _(act):
            ch = Chunks()
            hid, p, gate = Tally(hid_done), Tally(p_done), Tally(gate_done)

            def split(n):
                if ch.i is None and n >= N_ALL:
                    return
                act.wait_ge(loaded[n % RAW], ch.loaded(n))
                act.wait_ge(used, ch.count(n + 1))
                act.activation(w_hi[:, n % SLOTS, :], raw[:, n % RAW, :], ACT.Copy).then_inc(hi_done, 1)

            def chunk_used(n):
                act.wait_ge(used, ch.count(SLOTS + n + 1))

            def body(n0, chunks, work, hold_back=False):
                for j in range(chunks):
                    if j in work:
                        work[j](n0 + j)
                    if not (hold_back and j == chunks - 1):
                        split(n0 + j + SLOTS)

            def stage(n0, times, chunks, cmul, work, last_work=None, hold_back=False, gates=0):
                loops = times if last_work is None else times - 1
                with act.Fori(0, loops) as i:
                    ch.enter(i, chunks)
                    hid.enter(i, 4)
                    p.enter(i, cmul)
                    gate.enter(i, gates)
                    body(n0, chunks, work(i))
                ch.leave()
                for x in (hid, p, gate):
                    x.leave(loops)
                if last_work is not None:
                    body(n0 + loops * chunks, chunks, last_work, hold_back)

            def hid_split(tiles, width, src=None):
                for t in tiles:
                    act.wait_ge(hid_done, hid.at(1))
                    hid.up()
                    x = ta[:, t, 0:width] if src is None else src[:, t % 2, 0:width]
                    act.activation(hid_hi[:, t, 0:width], x, ACT.Copy).then_inc(hid_hi_done, 1)

            def square(norm, k):
                if k >= 4:
                    act.wait_ge(ssum_done, KD * (norm - 1) + k - 3)
                act.activation(tb[:, k % 4, first_of(norm):T], h[:, k, first_of(norm):T],
                               ACT.Square).then_inc(sq_done, 1)

            def hi_of_tile(norm, gain, k):
                act.activation(xn_hi[:, k, first_of(norm):T], h[:, k, first_of(norm):T], ACT.Copy,
                               scale=vecs[:, gain + k:gain + k + 1]).then_inc(xt_hi, 1)

            def square_tiles(norm, spread_before, q):
                def work(n):
                    for k in range(4 * q, 4 * q + 4):
                        act.wait_ge(spread_done, spread_before + k + 1)
                        square(norm, k)
                        if norm == 2:
                            hi_of_tile(norm, G_FFN2, k)
                        if norm == 3:
                            act.wait_ge(sq_done, KD * 2 + k + 1)
                            act.activation(h[:, k, META:T], h[:, k, META:T], ACT.Copy,
                                           scale=vecs[:, G_FINAL + k:G_FINAL + k + 1]).then_inc(hg_done, 1)
                return work

            def root(norm, x, out):
                act.wait_ge(root_in, norm + 1)
                act.activation(out, x, ACT.Sqrt).then_inc(root_done, 1)

            def load_root(norm):
                act.activation(warm[:, norm:norm + 1], ones[:, 0:1], ACT.Sqrt)

            def normalise_hi(norm, n0, between=None):
                for k in range(KD):
                    act.wait_ge(xt_done, KD * (norm - 1) + k + 1)
                    act.activation(xn_hi[:, k, :], ta[:, k % 4, :], ACT.Copy).then_inc(xt_hi, 1)
                    if k == HELD_BACK:
                        split(n0 + SLOTS - 1)
                    if between is not None and k in between:
                        between[k]()

            act.wait_ge(ones_done, 1)
            load_root(0)
            act.wait_ge(tok_set, 1)
            for t, (first, count) in enumerate(X_ROWS):
                act.wait_ge(x_in[t], 16 if t == 1 else 32)
                if t:
                    act.wait_ge(tok_sq, t)
                act.activation(squares_out[0:count, :], rows[0:count, t, :], ACT.Square,
                               accum_out=tok[0:count, 0, t:t + 1]).then_inc(tok_sq, 1)
            for n in range(SLOTS):
                split(n)
                if n == 0:
                    act.wait_ge(vecs_done, 1)
                    act.wait_ge(x_copied, 12)
                if n == 1:
                    root(0, tok[:, 1, :], tok[:, 3, :])
                for k in range(4 * n, 4 * n + 4):
                    hi_of_tile(0, G_FFN1, k)

            def sigmoids(dst, tiles, banks, width):
                def work(n):
                    chunk_used(n)
                    for t, b in zip(tiles, banks):
                        act.activation(dst[:, t, 0:width], bank[b][:, 0:width], ACT.Sigmoid).then_inc(sig_done, 1)
                return work

            def ffn(n0, first_token, next_norm, spread_before):
                width = T - first_token

                def gate_sigmoids(tiles):
                    def work(n):
                        for t in tiles:
                            act.wait_ge(gate_done, gate.at(1))
                            gate.up()
                            act.activation(tb[:, t, 0:width], ta[:, t, 0:width], ACT.Sigmoid).then_inc(sig_done, 1)
                    return work

                work = {
                    PROJ - 1: gate_sigmoids((0, 1)),
                    2 * PROJ - 1: lambda n: hid_split((0, 1), width),
                    3 * PROJ - 1: gate_sigmoids((2, 3)),
                    4 * PROJ - 1: lambda n: hid_split((2, 3), width),
                }
                last = dict(work)
                for q in range(4):
                    last[4 * PROJ + 2 * q + 1] = square_tiles(next_norm, spread_before + KD * (FFN_TURNS - 1), q)
                last[4 * PROJ] = lambda n: load_root(next_norm)
                stage(n0, FFN_TURNS, FFN_CHUNKS, 0, lambda i: work, last, hold_back=next_norm == 1, gates=4)

            ffn(N_FFN1, 0, 1, KD)
            root(1, rs[:, 0, :], rs[:, 2, :])

            def state_copy(g, dst, src):
                def copy():
                    act.wait_ge(turned, 14 + g)
                    act.activation(dst, src, ACT.Copy).then_inc(past_done, 1)
                return copy
            normalise_hi(1, N_POOL, {
                2: state_copy(0, conv_past[:].rearrange("p k c -> p (k c)"), bank[1][:, 0:256]),
                6: state_copy(1, pool_past[:, 0:4, :].rearrange("p k c -> p (k c)"), bank[2][:, 0:480]),
                10: state_copy(2, pool_past[:, 4:8, :].rearrange("p k c -> p (k c)"), bank[3][:, 0:480])})

            def place_past(a, g):
                if a:
                    act.wait_ge(hid_done, 4 * FFN_TURNS + 2 * a)
                for t in range(2):
                    act.activation(past_of(zbuf[:, t, META + SEQ:], SEG_Z, POOL_PAST),
                                   pool_past[:, 2 * g + t, :].rearrange("p (s c) -> p s c", s=SEQS), ACT.Copy)

            def place_z(a, g):
                for t in range(2):
                    zt = bank[Z_BANKS[a][t]]
                    act.activation(zbuf[:, t, 0:META + SEQ], zt[:, 0:META + SEQ], ACT.Copy)
                    act.activation(steps_of(zbuf[:, t, META + SEQ:], SEG_Z, POOL_PAST),
                                   zt[:, META + SEQ:T].rearrange("p (s c) -> p s c", s=SEQS),
                                   ACT.Copy).then_inc(z_done, 1)

            def keep_z(a, g):
                for t in range(2):
                    ins = act.activation(ztail[:, 2 * g + t, :], bank[Z_BANKS[a][t]][:, T - ZTAIL:T], ACT.Copy)
                ins.then_inc(z_kept, 1)

            def split_pooled(j):
                if j in POOL_SPLITS:
                    b = POOL_SPLITS[j]
                    hid_split((2 * (b % 2), 2 * (b % 2) + 1), LIVE, sums[pool_source(b)])

            act.wait_ge(past_done, 3)
            for j, (kind, a) in enumerate(POOL_PLAN):
                if kind == PROJ - 2:
                    place_past(a, POOL_ORDER[a])
                if kind == PROJ - 1:
                    chunk_used(N_POOL + j)
                    place_z(a, POOL_ORDER[a])
                    keep_z(a, POOL_ORDER[a])
                if POOL_SPLITS.get(j) == 3:
                    chunk_used(N_POOL + j)
                split_pooled(j)
                split(N_POOL + j + SLOTS)

            def conv_work(i):
                def place_v(tiles, banks):
                    def work(n):
                        chunk_used(n)
                        for t, b in zip(tiles, banks):
                            act.activation(tb[:, t, 0:CV], bank[b][:, 0:CV], ACT.Copy).then_inc(v_done, 1)
                            act.activation(
                                past_of(pbuf[:, t, CONV_PAST + SEQ:], SEG_C, CONV_PAST),
                                conv_past[:, bass.ds(i * 4 + t, 1), :].rearrange("p k (s c) -> p (k s) c", s=SEQS),
                                ACT.Copy).then_inc(placed, 1)
                    return work

                def keep_tails(tiles):
                    def work(n):
                        for t in tiles:
                            act.wait_ge(p_done, p.at(1))
                            p.up()
                            act.activation(ctail[:, bass.ds(i * 4 + t, 1), 0:CONV_PAST],
                                           pbuf[:, t:t + 1, SEQ:SEQ + CONV_PAST], ACT.Copy)
                            act.activation(
                                ctail[:, bass.ds(i * 4 + t, 1), CONV_PAST:].rearrange("p k (s c) -> p (k s) c", s=SEQS),
                                steps_of(pbuf[:, t, CONV_PAST + SEQ:], SEG_C, SEG_C - CONV_PAST),
                                ACT.Copy).then_inc(tails_done, 1)
                    return work
                return {
                    PROJ - 1: place_v((0, 1), (0, 1)),
                    2 * PROJ + 1: keep_tails((0, 1)),
                    3 * PROJ - 1: place_v((2, 3), (4, 5)),
                    4 * PROJ + 1: keep_tails((2, 3)),
                    5 * PROJ - 1: lambda n: hid_split((0, 1), LIVE),
                    6 * PROJ - 1: lambda n: hid_split((2, 3), LIVE),
                }
            stage(N_CONV, CONV_TURNS, CONV_CHUNKS, 4, conv_work)

            mix_work = {
                PROJ - 1: sigmoids(ta, (0, 1), (0, 1), LIVE),
                2 * PROJ - 1: sigmoids(ta, (2, 3), (2, 3), LIVE),
            }

            def sig_and_split(tiles, banks):
                def work(n):
                    sigmoids(tb, tiles, banks, LIVE)(n)
                    hid_split(tiles, LIVE)
                return work
            mix_work[3 * PROJ - 1] = sig_and_split((0, 1), (4, 5))
            mix_work[4 * PROJ - 1] = sig_and_split((2, 3), (6, 7))
            mix_last = dict(mix_work)
            mix_last[4 * PROJ] = lambda n: load_root(2)
            for q in range(4):
                mix_last[4 * PROJ + 2 * q + 1] = square_tiles(2, SPREAD_MIX + KD * MIX_TURNS, q)
            stage(N_MIX, MIX_TURNS, MIX_CHUNKS, 0, lambda i: mix_work, mix_last)

            root(2, rs[:, 0, META:T], rs[:, 2, META:T])

            def tail_copy(g):
                act.wait_ge(turned, 16 + g + 1)
                n_rows, dst = (ZTAIL, ztail_rows[:, 512 * g:512 * g + 512]) if g < 2 else (
                    CTAIL, ctail_rows[:, 512 * (g - 2):512 * (g - 2) + 512])
                act.activation(dst, bank[TAIL_BANKS[g]][0:n_rows, :], ACT.Copy).then_inc(tail_rows, 1)
            for g in range(6):
                tail_copy(g)

            ffn(N_FFN2, META, 3, SPREAD_FFN2 + KD)
            root(3, tok[:, 1, :], tok[:, 3, :])
            act.wait_ge(tails_stored, 16 * (4 + SEQS))
            act.wait_ge(rstd_tok, 1)
            for j in range(0, 12, 2):
                kg, t = j // 3, j % 3
                n_rows = Y_ROWS[t][1]
                act.wait_ge(turned, 22 + j + 1)
                act.activation(rows[0:n_rows, t, 512 * kg:512 * kg + 512], bank[j % 7][0:n_rows, :],
                               ACT.Copy, scale=tok[0:n_rows, 4, t:t + 1]).then_inc(rows_act, 1)

        @block.vector
        def _(dve):
            ch = Chunks()
            sig, hh, stp = Tally(sig_done), Tally(hid_hi_done), Tally(step)
            v, plc, pd, full = Tally(v_done), Tally(placed), Tally(p_done), Tally(bank_full)
            tallies = (sig, hh, stp, v, plc, pd, full)

            def split(n):
                if ch.i is None and n >= N_ALL:
                    return
                dve.wait_ge(hi_done, ch.count(n + 1))
                dve.tensor_tensor(w_lo[:, n % SLOTS, :], raw[:, n % RAW, :],
                                  w_hi[:, n % SLOTS, :].bitcast(F32), ALU.subtract).then_inc(lo_done, 1)

            def chunk_used(n):
                dve.wait_ge(used, ch.count(SLOTS + n + 1))

            def stepped(instruction):
                instruction.then_inc(step, 1)
                stp.up()
                dve.wait_ge(step, stp.at())

            def spread_ready(n, m):
                if m < 3:
                    full.up()
                    dve.wait_ge(bank_full, full.at())
                else:
                    chunk_used(n)

            def body(n0, chunks, work, hold_back=False):
                for j in range(chunks):
                    if j in work:
                        work[j](n0 + j)
                    if not (hold_back and j == chunks - 1):
                        split(n0 + j + SLOTS)

            def stage(n0, times, chunks, per, work, last_work=None, hold_back=False):
                loops = times if last_work is None else times - 1
                with dve.Fori(0, loops) as i:
                    ch.enter(i, chunks)
                    for x, k in zip(tallies, per):
                        x.enter(i, k)
                    body(n0, chunks, work(i))
                ch.leave()
                for x in tallies:
                    x.leave(loops)
                if last_work is not None:
                    body(n0 + loops * chunks, chunks, last_work, hold_back)

            def hid_split(tiles, width, src=None):
                for t in tiles:
                    dve.wait_ge(hid_hi_done, hh.at(1))
                    hh.up()
                    x = ta[:, t, 0:width] if src is None else src[:, t % 2, 0:width]
                    dve.tensor_tensor(hid_lo[:, t, 0:width], x, hid_hi[:, t, 0:width].bitcast(F32),
                                      ALU.subtract).then_inc(hid_lo_done, 1)

            def lo_of_tile(norm, gain, k):
                dve.wait_ge(xt_hi, KD * norm + k + 1)
                dve.scalar_tensor_tensor(out=xn_lo[:, k, first_of(norm):T], in0=h[:, k, first_of(norm):T],
                                         scalar=vecs[:, gain + k:gain + k + 1],
                                         in1=xn_hi[:, k, first_of(norm):T].bitcast(F32),
                                         op0=ALU.mult, op1=ALU.subtract).then_inc(xn_done, 1)

            def add_square(norm, k):
                first = first_of(norm)
                dve.wait_ge(sq_done, KD * (norm - 1) + k + 1)
                if k == 0:
                    dve.tensor_copy(ssum[:, first:T], tb[:, 0, first:T]).then_inc(ssum_done, 1)
                else:
                    dve.wait_ge(ssum_done, KD * (norm - 1) + k)
                    dve.tensor_tensor(ssum[:, first:T], ssum[:, first:T], tb[:, k % 4, first:T],
                                      ALU.add).then_inc(ssum_done, 1)

            def mean(x, v):
                return dve.tensor_scalar(v, x, 1.0 / D, EPS, ALU.mult, ALU.add)

            def inverse_root(norm, v, inverse, root, out):
                dve.wait_ge(root_in, norm + 1)
                stepped(dve.reciprocal(inverse, v))
                dve.wait_ge(root_done, norm + 1)
                stepped(dve.tensor_tensor(inverse, root, inverse, ALU.mult))
                stepped(dve.scalar_tensor_tensor(out=root, in0=inverse, scalar=-0.5, in1=root,
                                                 op0=ALU.mult, op1=ALU.mult))
                return dve.scalar_tensor_tensor(out=out, in0=root, scalar=1.5, in1=inverse,
                                                op0=ALU.add, op1=ALU.mult)

            def rms_of_channels(norm, b):
                dve.wait_ge(summed, norm)
                first = first_of(norm)
                mean(bank[b][:, 0:T - first], rs[:, 0, first:T]).then_inc(root_in, 1)
                stepped(inverse_root(norm, rs[:, 0, first:T], rs[:, 1, first:T], rs[:, 2, first:T],
                                     rstd[:, first:T]))

            def normalise(norm, gain, n0):
                for k in range(KD + 1):
                    if k < KD:
                        dve.scalar_tensor_tensor(out=ta[:, k % 4, :], in0=h[:, k, :],
                                                 scalar=vecs[:, gain + k:gain + k + 1], in1=rstd[:],
                                                 op0=ALU.mult, op1=ALU.mult).then_inc(xt_done, 1)
                    if k >= 1:
                        dve.wait_ge(xt_hi, KD * norm + k)
                        dve.tensor_tensor(xn_lo[:, k - 1, :], ta[:, (k - 1) % 4, :],
                                          xn_hi[:, k - 1, :].bitcast(F32), ALU.subtract).then_inc(xn_done, 1)
                    if k == HELD_BACK:
                        split(n0 + SLOTS - 1)

            dve.sem_inc(lo_done, RAW)
            dve.sem_inc(spread_done, KD)
            dve.memset(tok[:], 1.0).then_inc(tok_set, 1)
            for j in range(12):
                t, kg = j // 4, j % 4
                first, count = X_ROWS[t]
                dve.wait_ge(turned, j + 1)
                dve.tensor_copy(h[:, 4 * kg:4 * kg + 4, first:first + count],
                                bank[j % 8][:, 0:4 * count].rearrange("p (k c) -> p k c", k=4)).then_inc(x_copied, 1)
            dve.wait_ge(turned, 13)
            dve.tensor_copy(vecs[:], bank[4][:, 0:P]).then_inc(vecs_done, 1)
            dve.wait_ge(vecs_done, 1)
            for n in range(SLOTS):
                split(n)
                for k in range(4 * n, 4 * n + 4):
                    lo_of_tile(0, G_FFN1, k)
                if n == 0:
                    dve.wait_ge(tok_set, 1)
                    dve.wait_ge(tok_sq, 3)
                    mean(tok[:, 0, :], tok[:, 1, :]).then_inc(root_in, 1)
                if n == 1:
                    stepped(inverse_root(0, tok[:, 1, :], tok[:, 2, :], tok[:, 3, :], tok[:, 4, :]))
                    dve.wait_ge(ident_done, 1)
                    for t, (first, count) in enumerate(X_ROWS):
                        dve.tensor_scalar(tb[0:count, t, 0:count], ident[0:count, 0:count],
                                          tok[0:count, 4, t:t + 1], None, ALU.mult).then_inc(diag_done, 1)
            dve.wait_ge(rstd_in, 1)
            stepped(dve.tensor_copy(rstd[:], bank[5][:, 0:T]))

            def ffn(n0, first_token, next_norm):
                width = T - first_token

                def silu(tiles, banks):
                    def work(n):
                        chunk_used(n)
                        for t, b in zip(tiles, banks):
                            dve.tensor_tensor(ta[:, t, 0:width], bank[b][:, 0:width], rstd[:, first_token:T],
                                              ALU.mult).then_inc(gate_done, 1)
                        for t in tiles:
                            dve.wait_ge(sig_done, sig.at(1))
                            sig.up()
                            dve.tensor_tensor(ta[:, t, 0:width], ta[:, t, 0:width], tb[:, t, 0:width],
                                              ALU.mult).then_inc(step, 1)
                            stp.up()
                        for t in tiles:
                            dve.wait_ge(step, stp.at(-1))
                            dve.tensor_tensor(ta[:, t, 0:width], ta[:, t, 0:width], rstd[:, first_token:T],
                                              ALU.mult).then_inc(step, 1)
                            stp.up()
                    return work

                def times_up(tiles, banks):
                    def work(n):
                        chunk_used(n)
                        dve.wait_ge(step, stp.at())
                        for t, b in zip(tiles, banks):
                            dve.tensor_tensor(ta[:, t, 0:width], ta[:, t, 0:width], bank[b][:, 0:width],
                                              ALU.mult).then_inc(hid_done, 1)
                        hid_split(tiles, width)
                    return work

                def add_half(q, norm=None):
                    def work(n):
                        for m in range(4 * q, 4 * q + 4):
                            spread_ready(n, m % 4)
                            out = h[:, m, first_token:T]
                            dve.scalar_tensor_tensor(out=out, in0=bank[m % 8][:, 0:width], scalar=0.5,
                                                     in1=out, op0=ALU.mult, op1=ALU.add).then_inc(spread_done, 1)
                        if norm is not None:
                            for m in range(4 * q, 4 * q + 4):
                                add_square(norm, m)
                    return work

                work = {
                    PROJ - 1: silu((0, 1), (0, 1)),
                    2 * PROJ - 1: times_up((0, 1), (2, 3)),
                    3 * PROJ - 1: silu((2, 3), (4, 5)),
                    4 * PROJ - 1: times_up((2, 3), (6, 7)),
                }
                last = dict(work)
                for q in range(4):
                    work[4 * PROJ + 2 * q + 1] = add_half(q)
                    last[4 * PROJ + 2 * q + 1] = add_half(q, next_norm)
                stage(n0, FFN_TURNS, FFN_CHUNKS, (4, 4, 8, 0, 0, 0, 12), lambda i: work, last,
                      hold_back=next_norm == 1)

            ffn(N_FFN1, 0, 1)
            rms_of_channels(1, 0)
            normalise(1, G_MIX, N_POOL)

            def pool_group(a, g):
                window = WINDOWS[g]
                dve.wait_ge(hid_lo_done, 4 * FFN_TURNS + 2 * a)
                for t in range(2):
                    dve.wait_ge(z_done, 2 * a + t + 1)
                    src, d, w = zbuf[:, t, :], 1, 0
                    while d < window:
                        dst = sums[w][:, t, :]
                        stepped(dve.tensor_tensor(dst[:, 2 * d - 1:ZBUF], src[:, 2 * d - 1:ZBUF],
                                                  src[:, d - 1:ZBUF - d], ALU.add))
                        src, d, w = dst, 2 * d, 1 - w
                    z, out = zbuf[:, t, :], sums[w][:, t, :]
                    dve.scalar_tensor_tensor(out=out[:, 0:SEQ], in0=src[:, META:META + SEQ], scalar=1.0 / window,
                                             in1=z[:, META:META + SEQ], op0=ALU.mult, op1=ALU.subtract)
                    dve.scalar_tensor_tensor(
                        out=out[:, SEQ:LIVE].rearrange("p (s c) -> p s c", s=SEQS),
                        in0=steps_of(src[:, META + SEQ:], SEG_Z, POOL_PAST), scalar=1.0 / window,
                        in1=steps_of(z[:, META + SEQ:], SEG_Z, POOL_PAST), op0=ALU.mult,
                        op1=ALU.subtract).then_inc(hid_done, 1)

            def split_pooled(j):
                if j in POOL_SPLITS:
                    b = POOL_SPLITS[j]
                    hid_split((2 * (b % 2), 2 * (b % 2) + 1), LIVE, sums[pool_source(b)])

            for j, (kind, a) in enumerate(POOL_PLAN):
                if kind == PROJ - 1:
                    pool_group(a, POOL_ORDER[a])
                if POOL_SPLITS.get(j) != 3:
                    split_pooled(j)
                if kind == "map":
                    for m in range(4):
                        spread_ready(N_POOL + j, m)
                        tile = 4 * POOL_ORDER[a] + m
                        dve.tensor_scalar(ypool[:, tile, :], bank[MAP_BANKS[a][m]][:, 0:LIVE],
                                          vecs[:, G_SCALE + tile:G_SCALE + tile + 1], None,
                                          ALU.mult).then_inc(spread_done, 1)
                if POOL_SPLITS.get(j) == 3:
                    split_pooled(j)
                split(N_POOL + j + SLOTS)

            def spread_into(dst, first, q, high_first, norm=None):
                def work(n):
                    for m in range(4 * q, 4 * q + 4):
                        spread_ready(n, m % 4)
                        b = (m + 4) % 8 if high_first else m % 8
                        out = dst[:, m, first:first + LIVE]
                        dve.tensor_tensor(out, out, bank[b][:, 0:LIVE], ALU.add).then_inc(spread_done, 1)
                    if norm is not None:
                        for m in range(4 * q, 4 * q + 4):
                            add_square(norm, m)
                            lo_of_tile(norm, G_FFN2, m)
                return work

            dve.wait_ge(yconv_zero, 1)

            def conv_work(i):
                def convolve(tiles, banks):
                    def work(n):
                        chunk_used(n)
                        for t, b in zip(tiles, banks):
                            dve.wait_ge(v_done, v.at(1))
                            v.up()
                            dve.tensor_tensor(pbuf[:, t, 0:CONV_PAST + SEQ], tb[:, t, 0:CONV_PAST + SEQ],
                                              bank[b][:, 0:CONV_PAST + SEQ], ALU.mult)
                            dve.tensor_tensor(
                                steps_of(pbuf[:, t, CONV_PAST + SEQ:], SEG_C, CONV_PAST),
                                tb[:, t, CONV_PAST + SEQ:CV].rearrange("p (s c) -> p s c", s=SEQS),
                                bank[b][:, CONV_PAST + SEQ:CV].rearrange("p (s c) -> p s c", s=SEQS),
                                ALU.mult).then_inc(p_done, 1)
                        width = PBUF - CONV_PAST
                        for t in tiles:
                            pd.up()
                            plc.up()
                            dve.wait_ge(p_done, pd.at())
                            dve.wait_ge(placed, plc.at())

                            def tap(w, t=t):
                                return vecs[:, bass.ds(i * 4 + (G_CONV + 16 * w + t), 1)]
                            stepped(dve.tensor_scalar(tb[:, t, 0:width], pbuf[:, t, 0:width], tap(0), None, ALU.mult))
                            for w in (1, 2):
                                stepped(dve.scalar_tensor_tensor(
                                    out=tb[:, t, 0:width], in0=pbuf[:, t, w:w + width], scalar=tap(w),
                                    in1=tb[:, t, 0:width], op0=ALU.mult, op1=ALU.add))
                    return work

                def times_b(tiles, banks):
                    def work(n):
                        chunk_used(n)
                        for t, b in zip(tiles, banks):
                            dve.tensor_tensor(ta[:, t, 0:SEQ], tb[:, t, 0:SEQ], bank[b][:, 0:SEQ], ALU.mult)
                            y = steps_of(tb[:, t, SEQ:SEQ + SEQS * SEG_C], SEG_C, CONV_PAST)
                            dve.tensor_tensor(ta[:, t, SEQ:LIVE].rearrange("p (s c) -> p s c", s=SEQS), y,
                                              bank[b][:, SEQ:LIVE].rearrange("p (s c) -> p s c", s=SEQS),
                                              ALU.mult).then_inc(hid_done, 1)
                        hid_split(tiles, LIVE)
                    return work

                work = {
                    2 * PROJ - 1: convolve((0, 1), (2, 3)),
                    4 * PROJ - 1: convolve((2, 3), (6, 7)),
                    5 * PROJ - 1: times_b((0, 1), (0, 1)),
                    6 * PROJ - 1: times_b((2, 3), (2, 3)),
                }
                for q in range(4):
                    work[6 * PROJ + 2 * q + 1] = spread_into(yconv, 0, q, True)
                return work
            stage(N_CONV, CONV_TURNS, CONV_CHUNKS, (0, 4, 12, 4, 4, 4, 12), conv_work)

            def mix_work(i, norm=None):
                def gate_conv(tiles):
                    def work(n):
                        for t in tiles:
                            dve.wait_ge(sig_done, sig.at(1))
                            sig.up()
                            dve.tensor_tensor(ta[:, t:t + 1, 0:LIVE], ta[:, t:t + 1, 0:LIVE],
                                              yconv[:, bass.ds(i * 4 + t, 1), :], ALU.mult).then_inc(step, 1)
                            stp.up()
                    return work

                def gate_pool(tiles):
                    def work(n):
                        for t in tiles:
                            dve.wait_ge(sig_done, sig.at(1))
                            sig.up()
                            stepped(dve.tensor_tensor(tb[:, t:t + 1, 0:LIVE], tb[:, t:t + 1, 0:LIVE],
                                                      ypool[:, bass.ds(i * 4 + t, 1), :], ALU.mult))
                            dve.tensor_tensor(ta[:, t, 0:LIVE], ta[:, t, 0:LIVE], tb[:, t, 0:LIVE],
                                              ALU.add).then_inc(hid_done, 1)
                        hid_split(tiles, LIVE)
                    return work

                work = {
                    PROJ - 1: gate_conv((0, 1)),
                    2 * PROJ - 1: gate_conv((2, 3)),
                    3 * PROJ - 1: gate_pool((0, 1)),
                    4 * PROJ - 1: gate_pool((2, 3)),
                }
                for q in range(4):
                    work[4 * PROJ + 2 * q + 1] = spread_into(h, META, q, False, norm)
                return work
            stage(N_MIX, MIX_TURNS, MIX_CHUNKS, (8, 4, 8, 0, 0, 0, 12), mix_work, mix_work(MIX_TURNS - 1, 2))

            rms_of_channels(2, 4)
            ffn(N_FFN2, META, 3)

            dve.wait_ge(summed, 3)
            dve.tensor_scalar(tok[:, 1, 0:2], bank[7][:, 0:4].rearrange("p (t c) -> p t c", c=2)[:, :, 0],
                              1.0 / D, EPS, ALU.mult, ALU.add)
            mean(bank[7][0:SAMP, 4:5], tok[0:SAMP, 1, 2:3]).then_inc(root_in, 1)
            inverse_root(3, tok[:, 1, :], tok[:, 2, :], tok[:, 3, :], tok[:, 4, :]).then_inc(rstd_tok, 1)
            dve.wait_ge(tails_stored, 16 * (4 + SEQS))
            dve.wait_ge(rstd_tok, 1)
            for j in range(1, 12, 2):
                kg, t = j // 3, j % 3
                n_rows = Y_ROWS[t][1]
                dve.wait_ge(turned, 22 + j + 1)
                dve.tensor_scalar(rows[0:n_rows, t, 512 * kg:512 * kg + 512], bank[j % 7][0:n_rows, :],
                                  tok[0:n_rows, 4, t:t + 1], None, ALU.mult).then_inc(rows_dve, 1)


_INS = ['x_prompt', 'x_sample', 'state_conv', 'state_pool', 'meta_tokens', 'norm_ffn1', 'w_ffn1_gate',
        'w_ffn1_up', 'w_ffn1_down', 'norm_mix', 'w_in', 'conv_w', 'w_conv_out', 'w_pool_group',
        'pool_scale', 'w_o', 'norm_ffn2', 'w_ffn2_gate', 'w_ffn2_up', 'w_ffn2_down', 'norm_final']
_OUTS = [(1, SEQ, D), (SEQS, STEPS, D), (1, 1, CONV_PAST, D), (1, 1, POOL_PAST, D // 2),
         (1, SEQS, CONV_PAST, D), (1, SEQS, POOL_PAST, D // 2)]


def kernel(**inputs):
    import numpy as np
    import concourse.bacc as bacc
    from concourse.bass_utils import run_bass_kernel_spmd

    nc = bacc.Bacc("TRN2", target_bir_lowering=False, num_devices=1)
    arrays, args = {}, []
    for name in _INS:
        a = np.ascontiguousarray(inputs[name])
        arrays[f"in_{name}"] = a
        args.append(nc.dram_tensor(f"in_{name}", a.shape, mybir.dt.from_np(a.dtype), kind="ExternalInput").ap())
    for i, shape in enumerate(_OUTS):
        args.append(nc.dram_tensor(f"out_{i}", shape, F32, kind="ExternalOutput").ap())
    build(nc, *args)
    r = run_bass_kernel_spmd(nc, [arrays], core_ids=[0])
    return tuple(r.results[0][f"out_{i}"] for i in range(len(_OUTS)))
```

```python
from contextlib import ExitStack

import concourse.bass as bass
from concourse import mybir

F32 = mybir.dt.float32
F32R = mybir.dt.float32r
ALU = mybir.AluOpType
ACT = mybir.ActivationFunctionType

P = 128
D = 2048
F = 5632
KD = D // P
META, SEQ = 16, 256
SEQS, STEPS = 8, 8
SAMP = SEQS * STEPS
T = META + SEQ + SAMP
LIVE = SEQ + SAMP
CONV_PAST = 2
CV = CONV_PAST + LIVE
POOL_PAST = 15
WINDOWS = (2, 4, 8, 16)
EPS = 1e-6

CHUNK = 1024
RAW = 8
SLOTS = 4
PROJ = 4
SPREAD = 8
SPREAD_PLAN = ((0, 0), (1, 0), (0, 1), (1, 1), (2, 0), (2, 1), (3, 0), (3, 1))
SPREAD_ENDS = (2, 3, 5, 7)

FFN_TURNS = F // 512
FFN_CHUNKS = 4 * PROJ + SPREAD
CONV_TURNS = D // 512
CONV_CHUNKS = 6 * PROJ + SPREAD
MIX_TURNS = D // 512
MIX_CHUNKS = 4 * PROJ + SPREAD
POOL_ORDER = (3, 2, 1, 0)
POOL_CHUNKS = 4 * (PROJ + 1)

SUM_AT = 10
PRODUCTS_FIRST, PRODUCTS_THEN = 9, 9

N_FFN1 = 0
N_POOL = N_FFN1 + FFN_TURNS * FFN_CHUNKS
N_CONV = N_POOL + POOL_CHUNKS
N_MIX = N_CONV + CONV_TURNS * CONV_CHUNKS
N_FFN2 = N_MIX + MIX_TURNS * MIX_CHUNKS
N_ALL = N_FFN2 + FFN_TURNS * FFN_CHUNKS

B0, C0, V0, Z0, GC0, GP0 = 0, D, 2 * D, 3 * D, 3 * D + D // 2, 4 * D + D // 2

G_FFN1, G_MIX, G_FFN2, G_FINAL, G_SCALE, G_CONV = 0, 16, 32, 48, 64, 80
GAINS = (G_FFN1, G_MIX, G_FFN2, G_FINAL)

SEG_C = CONV_PAST + STEPS
PBUF = CONV_PAST + SEQ + SEQS * SEG_C
SEG_Z = POOL_PAST + STEPS
ZBUF = META + SEQ + SEQS * SEG_Z
CTAIL = CONV_PAST + SEQS * CONV_PAST
ZTAIL = POOL_PAST + SAMP

SPREAD_MIX = KD * FFN_TURNS + KD + KD * CONV_TURNS
SPREAD_FFN2 = SPREAD_MIX + KD * MIX_TURNS

POOL_PLAN = [(c, a) for a in (0, 1) for c in range(PROJ)] + [("map", 0)]
POOL_PLAN += [(c, a) for a in (2, 3) for c in range(PROJ)] + [("map", a) for a in (1, 2, 3)]
TAIL_BANKS = (2, 3, 5, 6, 7, 4)
Z_BANKS = ((0, 1), (2, 3), (0, 1), (2, 3))
MAP_BANKS = ((4, 5, 6, 7), (4, 5, 6, 7), (0, 1, 2, 3), (4, 5, 6, 7))
POOL_SPLITS = {4: 0, 8: 1, 13: 2, 17: 3}


def pool_source(a):
    return (POOL_ORDER[a] + 1) % 2


def first_of(norm):
    return META if norm >= 2 else 0


class Tally:

    def __init__(self, sem, start=0):
        self.sem, self.n, self.turns, self.per, self.first = sem, start, None, 0, 0

    def up(self, k=1):
        self.n += k

    def at(self, k=0):
        return self.n + k if self.turns is None else self.turns + (self.n + k)

    def enter(self, i, per):
        self.per, self.turns, self.first = per, i * per if per else None, self.n

    def leave(self, times):
        assert self.n - self.first == self.per, (self.sem, self.n - self.first, self.per)
        self.n, self.turns = self.first + times * self.per, None


class Chunks:

    def __init__(self):
        self.i, self.chunks = None, 0

    def enter(self, i, chunks):
        self.i, self.chunks = i, chunks

    def leave(self):
        self.i = None

    def count(self, x):
        return x if self.i is None else self.i * self.chunks + x

    def loaded(self, n):
        x = 16 * (n // RAW + 1)
        return x if self.i is None else self.i * (16 * self.chunks // RAW) + x


def build(nc, x_prompt, x_sample, state_conv, state_pool, meta_tokens, norm_ffn1, w_ffn1_gate,
          w_ffn1_up, w_ffn1_down, norm_mix, w_in, conv_w, w_conv_out, w_pool_group, pool_scale,
          w_o, norm_ffn2, w_ffn2_gate, w_ffn2_up, w_ffn2_down, norm_final,
          y_prompt, y_sample, new_conv_prompt, new_pool_prompt, new_conv_sample, new_pool_sample):
    with ExitStack() as ctx:
        def sb(name, shape, dt=F32):
            return ctx.enter_context(nc.sbuf_tensor(name, shape, dt))

        def sem(name):
            return ctx.enter_context(nc.semaphore(name))

        h = sb("h", [P, KD, T])
        xn_hi = sb("xn_hi", [P, KD, T], F32R)
        xn_lo = sb("xn_lo", [P, KD, T], F32R)
        hid_hi = sb("hid_hi", [P, 4, T], F32R)
        hid_lo = sb("hid_lo", [P, 4, T], F32R)
        raw = sb("raw", [P, RAW, CHUNK])
        w_hi = sb("w_hi", [P, SLOTS, CHUNK], F32R)
        w_lo = sb("w_lo", [P, SLOTS, CHUNK], F32R)
        acc = sb("acc", [P, 2, KD, LIVE])
        ta = sb("ta", [P, 4, T])
        tb = sb("tb", [P, 4, T])
        pbuf = sb("pbuf", [P, 4, PBUF])
        ssum = sb("ssum", [P, T])
        rstd = sb("rstd", [P, T])
        tok = sb("tok", [P, 5, 3])
        warm = sb("warm", [P, 4])
        vecs_in = sb("vecs_in", [P, P])
        vecs = sb("vecs", [P, P])
        conv_past = sb("conv_past", [P, KD, SEQS * CONV_PAST])
        pool_past = sb("pool_past", [P, KD // 2, SEQS * POOL_PAST])
        ctail = sb("ctail", [P, KD, CTAIL])
        ztail = sb("ztail", [P, KD // 2, ZTAIL])
        ident = sb("ident", [P, P])
        ones = sb("ones", [P, P])
        bank = [ctx.enter_context(nc.psum_tensor(f"bank{b}", [P, 512], F32)) for b in range(8)]

        yconv, ypool = acc[:, 0], acc[:, 1]
        acc_flat = acc[:].rearrange("p a k t -> p (a k t)")
        rows = acc_flat[:, 0:3 * D].rearrange("p (t d) -> p t d", t=3)
        squares_out = acc_flat[:, 3 * D:4 * D]
        conv_rows = acc_flat[0:SEQS * CONV_PAST, 3 * D:4 * D]
        pool_rows = acc_flat[0:SEQS * POOL_PAST, 4 * D:4 * D + D // 2]
        ctail_rows = acc_flat[0:CTAIL, 0:D]
        ztail_rows = acc_flat[0:ZTAIL, D:D + D // 2]
        flat_p = pbuf[:].rearrange("p a c -> p (a c)")
        zbuf = flat_p[:, 0:2 * ZBUF].rearrange("p (a c) -> p a c", a=2)
        rs = flat_p[:, 0:3 * T].rearrange("p (a c) -> p a c", a=3)
        sums = [x[:].rearrange("p a c -> p (a c)")[:, 0:2 * ZBUF].rearrange("p (a c) -> p a c", a=2)
                for x in (ta, tb)]
        X_ROWS = ((0, P), (P, P), (2 * P, T - 2 * P))
        Y_ROWS = ((META, P), (META + P, P), (META + SEQ, SAMP))

        def steps_of(row, seg, past):
            return row.rearrange("p (s c) -> p s c", c=seg)[:, :, past:seg]

        def past_of(row, seg, past):
            return row.rearrange("p (s c) -> p s c", c=seg)[:, :, 0:past]

        x_in = [sem(f"x_in{t}") for t in range(3)]
        vecs_in_done, states_in = sem("vecs_in_done"), sem("states_in")
        tok_set = sem("tok_set")
        loaded = [sem(f"loaded{s}") for s in range(RAW)]
        hi_done = sem("hi_done")
        lo_done = sem("lo_done")
        used = sem("used")
        ident_zero, ident_done, ones_done = sem("ident_zero"), sem("ident_done"), sem("ones_done")
        yconv_zero = sem("yconv_zero")
        turned = sem("turned")
        summed = sem("summed")
        x_copied = sem("x_copied")
        vecs_done = sem("vecs_done")
        past_done = sem("past_done")
        tok_sq = sem("tok_sq")
        diag_done = sem("diag_done")
        rstd_in = sem("rstd_in")
        sq_done = sem("sq_done")
        ssum_done = sem("ssum_done")
        root_in, root_done = sem("root_in"), sem("root_done")
        rstd_done = sem("rstd_done")
        xt_hi = sem("xt_hi")
        xn_done = sem("xn_done")
        gate_done = sem("gate_done")
        sig_done = sem("sig_done")
        placed = sem("placed")
        z_past = sem("z_past")
        z_done = sem("z_done")
        z_kept = sem("z_kept")
        tails_done = sem("tails_done")
        step = sem("step")
        p_done = sem("p_done")
        hid_done = sem("hid_done")
        hid_hi_done = sem("hid_hi_done")
        hid_lo_done = sem("hid_lo_done")
        spread_done = sem("spread_done")
        tail_rows = sem("tail_rows")
        hg_done = sem("hg_done")
        rows_act, rows_dve = sem("rows_act"), sem("rows_dve")
        rstd_tok = sem("rstd_tok")
        bank_full = sem("bank_full")
        tails_stored, y_stored = sem("tails_stored"), sem("y_stored")
        slot_seen_free = sem("slot_seen_free")

        def proj_view(w, c, col):
            return w.rearrange("(k p) n -> p k n", p=P)[:, 4 * c:4 * c + 4, bass.ds(col, 256)]

        def spread_view(w, k, q):
            return w.rearrange("(k p) n -> p k n", p=P)[:, bass.ds(k, 2), 512 * q:512 * q + 512]

        block = ctx.enter_context(nc.Block())

        @block.sync
        def _(sp):
            ch = Chunks()
            sp.dma_start(rows[0:META, 0, :], meta_tokens).then_inc(x_in[0], 16)
            sp.dma_start(rows[META:P, 0, :], x_prompt[0, 0:P - META, :]).then_inc(x_in[0], 16)
            sp.dma_start(rows[:, 1, :], x_prompt[0, P - META:2 * P - META, :]).then_inc(x_in[1], 16)
            flat = "l d -> (l d)"
            for v, (src, n) in enumerate((
                    (norm_ffn1.rearrange(flat), 16), (norm_mix.rearrange(flat), 16),
                    (norm_ffn2.rearrange(flat), 16), (norm_final, 16),
                    (pool_scale.rearrange(flat), 16), (conv_w.rearrange("l w d -> (l w d)"), 48))):
                sp.dma_start(vecs_in[16 * v:16 * v + n, :],
                             src.rearrange("(k p) -> k p", p=P)).then_inc(vecs_in_done, 16)
            sp.dma_start(rows[0:META, 2, :], x_prompt[0, 2 * P - META:SEQ, :]).then_inc(x_in[2], 16)
            sp.dma_start(rows[META:META + SAMP, 2, :],
                         x_sample.rearrange("b s d -> (b s) d")).then_inc(x_in[2], 16)

            def load(n, src, k_tiles, at_start=False):
                sp.wait_ge(lo_done, ch.count(n + 1))
                if at_start:
                    sp.sem_inc(slot_seen_free, 1)
                sp.dma_start(raw[:, n % RAW, :].rearrange("p (k n) -> p k n", k=k_tiles),
                             src).then_inc(loaded[n % RAW], 16)

            def blocks(n0, times, chunks, projections, spread_over):
                assert chunks % RAW == 0
                with sp.Fori(0, times) as i:
                    ch.enter(i, chunks)
                    col, k = sp.snap(i * 512), sp.snap(i * 4)
                    n = n0
                    for w, first in projections:
                        for c in range(PROJ):
                            load(n, proj_view(w, c, col + first), 4, first + c == 0)
                            n += 1
                    for q, half in SPREAD_PLAN:
                        load(n, spread_view(spread_over, k + 2 * half, q), 2)
                        n += 1
                ch.leave()

            def ffn(n0, gate, up, down):
                blocks(n0, FFN_TURNS, FFN_CHUNKS, ((gate, 0), (up, 0), (gate, 256), (up, 256)), down)

            win = w_in[0]
            ffn(N_FFN1, w_ffn1_gate[0], w_ffn1_up[0], w_ffn1_down[0])
            for j, (kind, a) in enumerate(POOL_PLAN):
                g = POOL_ORDER[a]
                if kind == "map":
                    load(N_POOL + j, w_pool_group[0, g].rearrange("(k p) n -> p k n", p=P), 2)
                else:
                    load(N_POOL + j, proj_view(win, kind, Z0 + 256 * g), 4)
            blocks(N_CONV, CONV_TURNS, CONV_CHUNKS,
                   [(win, col) for col in (V0, C0, V0 + 256, C0 + 256, B0, B0 + 256)], w_conv_out[0])
            blocks(N_MIX, MIX_TURNS, MIX_CHUNKS,
                   [(win, col) for col in (GC0, GC0 + 256, GP0, GP0 + 256)], w_o[0])
            ffn(N_FFN2, w_ffn2_gate[0], w_ffn2_up[0], w_ffn2_down[0])

            for j in range(12):
                kg, t = j // 3, j % 3
                sp.wait_ge(rows_dve if j % 2 else rows_act, j // 2 + 1)
                dst = y_prompt[0, t * P:(t + 1) * P, :] if t < 2 else y_sample.rearrange("b s d -> (b s) d")
                sp.dma_start(dst[:, 512 * kg:512 * kg + 512],
                             rows[0:Y_ROWS[t][1], t, 512 * kg:512 * kg + 512]).then_inc(y_stored, 16)
            sp.wait_ge(y_stored, 16 * 12)

        @block.gpsimd
        def _(pool):
            pool.memset(ident[:], 0.0).then_inc(ident_zero, 1)
            pool.wait_ge(ident_zero, 1)
            pool.affine_select(out=ident[:], in_=ident[:], compare_op=ALU.not_equal, fill=1.0, base=0,
                               pattern=[[-1, P]], channel_multiplier=1).then_inc(ident_done, 1)
            pool.memset(ones[:], 1.0).then_inc(ones_done, 1)
            pool.wait_ge(tok_sq, 3)
            pool.wait_ge(x_copied, 12)
            pool.dma_start(conv_rows, state_conv.rearrange("l b w d -> (l b w) d")).then_inc(states_in, 16)
            pool.dma_start(pool_rows, state_pool.rearrange("l b w d -> (l b w) d")).then_inc(states_in, 16)
            pool.memset(yconv, 0.0).then_inc(yconv_zero, 1)
            pool.dma_start(new_pool_sample[0, :, 0:POOL_PAST - STEPS, :],
                           state_pool[0, :, STEPS:POOL_PAST, :]).then_inc(tails_stored, 16)
            pool.wait_ge(tail_rows, 6)
            pool.dma_start(new_conv_prompt[0, 0], ctail_rows[0:CONV_PAST, :]).then_inc(tails_stored, 16)
            pool.dma_start(new_conv_sample[0].rearrange("b w d -> (b w) d"),
                           ctail_rows[CONV_PAST:CTAIL, :]).then_inc(tails_stored, 16)
            pool.dma_start(new_pool_prompt[0, 0], ztail_rows[0:POOL_PAST, :]).then_inc(tails_stored, 16)
            for s in range(SEQS):
                r = POOL_PAST + STEPS * s
                pool.dma_start(new_pool_sample[0, s, POOL_PAST - STEPS:POOL_PAST, :],
                               ztail_rows[r:r + STEPS, :]).then_inc(tails_stored, 16)

        @block.tensor
        def _(pe):
            ch = Chunks()
            hid, spr, p = Tally(hid_lo_done), Tally(spread_done, KD), Tally(p_done)
            LOW, HIGH = (0, 1, 2, 3), (4, 5, 6, 7)

            def three_passes(out, slot, cols, x_hi, x_lo, start, stop):
                pe.matmul(out, w_hi[:, slot, cols], x_hi, start=start, stop=False)
                pe.matmul(out, w_hi[:, slot, cols], x_lo, start=False, stop=False)
                return pe.matmul(out, w_lo[:, slot, cols], x_hi, start=False, stop=stop)

            def project(n, banks, first_token, norm=None, between=None):
                for c in range(PROJ):
                    pe.wait_ge(lo_done, ch.count(RAW + n + c + 1))
                    for kk in range(4):
                        k = 4 * c + kk
                        if between is not None and k == between[0]:
                            between[1]()
                        if norm is not None:
                            pe.wait_ge(xn_done, KD * norm + k + 1)
                        for t, b in enumerate(banks):
                            col = kk * 256 + t * P
                            last = three_passes(bank[b][:, 0:T - first_token], (n + c) % SLOTS,
                                                slice(col, col + P), xn_hi[:, k, first_token:T],
                                                xn_lo[:, k, first_token:T], k == 0, k == KD - 1)
                    last.then_inc(used, 1)

            def spread(n, banks, width, tiles, first, last, ready):
                if ready:
                    pe.wait_ge(hid_lo_done, hid.at(2))
                    hid.up(2)
                pe.wait_ge(lo_done, ch.count(RAW + n + 1))
                for m, b in enumerate(banks):
                    for kk, k in enumerate(tiles):
                        col = kk * 512 + m * P
                        ins = three_passes(bank[b][:, 0:width], n % SLOTS, slice(col, col + P),
                                           hid_hi[:, k, 0:width], hid_lo[:, k, 0:width],
                                           first and kk == 0, last and kk == 1)
                    if last and m < 3:
                        ins.then_inc(bank_full, 1)
                ins.then_inc(used, 1)

            def spread_all(n, width):
                for j, (q, half) in enumerate(SPREAD_PLAN):
                    if q == 1 and half == 0:
                        pe.wait_ge(hid_done, hid.at(2))
                    if q >= 2 and half == 0:
                        pe.wait_ge(spread_done, spr.at(4 * (q - 1)))
                    spread(n + j, (LOW, HIGH)[q % 2], width, (2 * half, 2 * half + 1), half == 0, half == 1,
                           ready=q == 0)
                spr.up(KD)

            def loop(times, chunks, cmul, body):
                with pe.Fori(0, times) as i:
                    ch.enter(i, chunks)
                    hid.enter(i, 4)
                    spr.enter(i, KD)
                    p.enter(i, cmul)
                    body()
                ch.leave()
                for x in (hid, spr, p):
                    x.leave(times)

            def sum_squares(norm, b):
                pe.wait_ge(ssum_done, KD * norm)
                pe.matmul(bank[b][:, 0:T - first_of(norm)], ones[:], ssum[:, first_of(norm):T],
                          start=True, stop=True).then_inc(summed, 1)

            def keep_busy(products):
                for _ in range(products):
                    pe.matmul(bank[7][:, 0:P], ident[:], ident[:], start=True, stop=True)

            pe.wait_ge(ident_done, 1)
            keep_busy(PRODUCTS_FIRST)
            for t, (first, count) in enumerate(X_ROWS):
                if t == 2:
                    pe.wait_ge(vecs_in_done, 16 * 6)
                    pe.wait_ge(x_copied, 5)
                    pe.transpose(bank[4][:, 0:P], vecs_in[:], ident[:]).then_inc(turned, 1)
                pe.wait_ge(x_in[t], 16 if t == 1 else 32)
                for kg in range(4):
                    if t == 2:
                        pe.wait_ge(x_copied, kg + 1)
                    for k in range(4):
                        last = pe.transpose(bank[(4 * t + kg) % 8][:, k * count:(k + 1) * count],
                                            rows[0:count, t, (4 * kg + k) * P:(4 * kg + k + 1) * P],
                                            ident[0:count, 0:count])
                    last.then_inc(turned, 1)

            def spread_rstd():
                pe.wait_ge(ones_done, 1)
                pe.wait_ge(diag_done, 3)
                for t, (first, count) in enumerate(X_ROWS):
                    last = pe.matmul(bank[5][:, first:first + count], ones[0:count, :], tb[0:count, t, 0:count],
                                     start=True, stop=True)
                last.then_inc(rstd_in, 1)

            pe.wait_ge(x_copied, 8)
            keep_busy(PRODUCTS_THEN)
            pe.sem_inc(used, SLOTS)
            pe.wait_ge(x_copied, 12)

            def ffn_block(n, first_token, norm=None, between=None):
                pe.wait_ge(spread_done, spr.at(-4))
                project(n, (0, 1), first_token, norm, between)
                if norm == 2:
                    pe.wait_ge(tail_rows, 2)
                project(n + PROJ, (2, 3), first_token)
                pe.wait_ge(spread_done, spr.at())
                if norm == 2:
                    pe.wait_ge(tail_rows, 6)
                project(n + 2 * PROJ, (4, 5), first_token)
                project(n + 3 * PROJ, (6, 7), first_token)
                spread_all(n + 4 * PROJ, T - first_token)

            def ffn(n0, first_token, norm, between):
                ffn_block(n0, first_token, norm, between)
                loop(FFN_TURNS - 1, FFN_CHUNKS, 0, lambda: ffn_block(n0 + FFN_CHUNKS, first_token))

            ffn(N_FFN1, 0, 0, (SUM_AT - 2, spread_rstd))

            def sum_and_states():
                pe.wait_ge(spread_done, spr.at())
                sum_squares(1, 4)
                pe.wait_ge(states_in, 32)
                for k in range(KD):
                    last = pe.transpose(bank[5][:, 16 * k:16 * k + 16], conv_rows[:, k * P:(k + 1) * P],
                                        ident[0:16, 0:16])
                last.then_inc(turned, 1)
                for g in range(2):
                    for k in range(4):
                        col = (4 * g + k) * P
                        last = pe.transpose(bank[6 + g][:, 120 * k:120 * k + 120], pool_rows[:, col:col + P],
                                            ident[0:120, 0:120])
                    last.then_inc(turned, 1)

            pe.wait_ge(spread_done, spr.at(-4))
            for j, (kind, a) in enumerate(POOL_PLAN):
                if kind == 0:
                    if a >= 2:
                        pe.wait_ge(z_done, 2 * (a - 1))
                    project(N_POOL + j, Z_BANKS[a], 0, 1 if a == 0 else None,
                            (SUM_AT, sum_and_states) if a == 0 else None)
                elif kind == "map":
                    if a == 0:
                        pe.wait_ge(root_in, 2)
                        pe.wait_ge(past_done, 3)
                    if a == 2:
                        pe.wait_ge(z_done, 8)
                    if a in (1, 3):
                        pe.wait_ge(spread_done, spr.at(0 if a == 1 else -4))
                    spread(N_POOL + j, MAP_BANKS[a], LIVE, (2 * (a % 2), 2 * (a % 2) + 1), True, True, ready=True)
                    spr.up(4)

            def conv_body():
                n = N_CONV
                pe.wait_ge(spread_done, spr.at(-4))
                project(n, (0, 1), META - CONV_PAST)
                project(n + PROJ, (2, 3), META - CONV_PAST)
                pe.wait_ge(spread_done, spr.at())
                project(n + 2 * PROJ, (4, 5), META - CONV_PAST)
                project(n + 3 * PROJ, (6, 7), META - CONV_PAST)
                pe.wait_ge(p_done, p.at(2))
                project(n + 4 * PROJ, (0, 1), META)
                pe.wait_ge(p_done, p.at(4))
                p.up(4)
                project(n + 5 * PROJ, (4, 5), META)
                spread_all(n + 6 * PROJ, LIVE)
            loop(CONV_TURNS, CONV_CHUNKS, 4, conv_body)

            def mix_body():
                n = N_MIX
                pe.wait_ge(spread_done, spr.at(-4))
                project(n, (0, 1), META)
                project(n + PROJ, (2, 3), META)
                pe.wait_ge(spread_done, spr.at())
                project(n + 2 * PROJ, (4, 5), META)
                project(n + 3 * PROJ, (6, 7), META)
                spread_all(n + 4 * PROJ, LIVE)
            loop(MIX_TURNS, MIX_CHUNKS, 0, mix_body)

            def sum_and_tails():
                sum_squares(2, 4)
                pe.wait_ge(tails_done, KD)
                for g in range(2):
                    for k in range(4):
                        last = pe.transpose(bank[2 + g][0:ZTAIL, k * P:(k + 1) * P], ztail[:, 4 * g + k, :], ident[:])
                    last.then_inc(turned, 1)
                for g in range(4):
                    if g == 3:
                        pe.wait_ge(root_in, 3)
                    for k in range(4):
                        last = pe.transpose(bank[TAIL_BANKS[2 + g]][0:CTAIL, k * P:(k + 1) * P],
                                            ctail[:, 4 * g + k, :], ident[:])
                    last.then_inc(turned, 1)

            ffn(N_FFN2, META, 2, (SUM_AT, sum_and_tails))

            for j in range(12):
                kg, (first, count) = j // 3, Y_ROWS[j % 3]
                if j % 3 == 0:
                    pe.wait_ge(hg_done, 4 * kg + 4)
                if j == 0:
                    pe.wait_ge(spread_done, spr.at(-4))
                if j == 4:
                    pe.wait_ge(spread_done, spr.at())
                if j == 7:
                    pe.wait_ge(ssum_done, KD * 3)
                    for t, (at, n) in enumerate(Y_ROWS):
                        last = pe.matmul(bank[7][0:n, 2 * t:2 * t + 2], ssum[:, at:at + n], ones[:, 0:2],
                                         start=True, stop=True)
                    last.then_inc(summed, 1)
                if j >= 7:
                    pe.wait_ge(rows_act if j % 2 else rows_dve, (j - 7) // 2 + 1)
                for k in range(4):
                    last = pe.transpose(bank[j % 7][0:count, k * P:(k + 1) * P],
                                        h[:, 4 * kg + k, first:first + count], ident[:])
                last.then_inc(turned, 1)

        @block.scalar
        def _(act):
            ch = Chunks()
            hid, p, gate = Tally(hid_done), Tally(p_done), Tally(gate_done)

            def split(n):
                if ch.i is None and n >= N_ALL:
                    return
                act.wait_ge(loaded[n % RAW], ch.loaded(n))
                act.wait_ge(used, ch.count(n + 1))
                act.activation(w_hi[:, n % SLOTS, :], raw[:, n % RAW, :], ACT.Copy).then_inc(hi_done, 1)

            def chunk_used(n):
                act.wait_ge(used, ch.count(SLOTS + n + 1))

            def body(n0, chunks, work):
                for j in range(chunks):
                    if j in work:
                        work[j](n0 + j)
                    split(n0 + j + SLOTS)

            def stage(n0, times, chunks, cmul, work, last_work=None, gates=0):
                loops = times if last_work is None else times - 1
                with act.Fori(0, loops) as i:
                    ch.enter(i, chunks)
                    hid.enter(i, 4)
                    p.enter(i, cmul)
                    gate.enter(i, gates)
                    body(n0, chunks, work(i))
                ch.leave()
                for x in (hid, p, gate):
                    x.leave(loops)
                if last_work is not None:
                    body(n0 + loops * chunks, chunks, last_work)

            def hid_split(tiles, width, src=None):
                for t in tiles:
                    act.wait_ge(hid_done, hid.at(1))
                    hid.up()
                    x = ta[:, t, 0:width] if src is None else src[:, t % 2, 0:width]
                    act.activation(hid_hi[:, t, 0:width], x, ACT.Copy).then_inc(hid_hi_done, 1)

            def square(norm, k):
                if k >= 4:
                    act.wait_ge(ssum_done, KD * (norm - 1) + k - 3)
                act.activation(tb[:, k % 4, first_of(norm):T], h[:, k, first_of(norm):T],
                               ACT.Square).then_inc(sq_done, 1)

            def hi_of_tile(norm, gain, k):
                act.activation(xn_hi[:, k, first_of(norm):T], h[:, k, first_of(norm):T], ACT.Copy,
                               scale=vecs[:, gain + k:gain + k + 1]).then_inc(xt_hi, 1)

            def square_tiles(norm, spread_before, q):
                def work(n):
                    for k in range(4 * q, 4 * q + 4):
                        act.wait_ge(spread_done, spread_before + k + 1)
                        square(norm, k)
                        if norm < 3:
                            hi_of_tile(norm, GAINS[norm], k)
                        else:
                            act.wait_ge(sq_done, KD * 2 + k + 1)
                            act.activation(h[:, k, META:T], h[:, k, META:T], ACT.Copy,
                                           scale=vecs[:, G_FINAL + k:G_FINAL + k + 1]).then_inc(hg_done, 1)
                return work

            def root(norm, x, out):
                act.wait_ge(root_in, norm + 1)
                act.activation(out, x, ACT.Sqrt).then_inc(root_done, 1)

            def load_root(norm):
                act.activation(warm[:, norm:norm + 1], ones[:, 0:1], ACT.Sqrt)

            act.wait_ge(ones_done, 1)
            load_root(0)
            act.wait_ge(tok_set, 1)
            for t, (first, count) in enumerate(X_ROWS):
                act.wait_ge(x_in[t], 16 if t == 1 else 32)
                if t:
                    act.wait_ge(tok_sq, t)
                act.activation(squares_out[0:count, :], rows[0:count, t, :], ACT.Square,
                               accum_out=tok[0:count, 0, t:t + 1]).then_inc(tok_sq, 1)
            for n in range(SLOTS):
                split(n)
                if n == 0:
                    act.wait_ge(vecs_done, 1)
                act.wait_ge(x_copied, 8 + n + 1)
                if n == 1:
                    root(0, tok[:, 1, :], tok[:, 3, :])
                for k in range(4 * n, 4 * n + 4):
                    hi_of_tile(0, G_FFN1, k)

            def sigmoids(src, dst, tiles, width):
                def work(n):
                    for t in tiles:
                        act.wait_ge(gate_done, gate.at(1))
                        gate.up()
                        act.activation(dst[:, t, 0:width], src[:, t, 0:width], ACT.Sigmoid).then_inc(sig_done, 1)
                return work

            def ffn(n0, first_token, next_norm, spread_before):
                width = T - first_token
                work = {
                    PROJ - 1: sigmoids(ta, tb, (0, 1), width),
                    2 * PROJ - 1: lambda n: hid_split((0, 1), width),
                    3 * PROJ - 1: sigmoids(ta, tb, (2, 3), width),
                    4 * PROJ - 1: lambda n: hid_split((2, 3), width),
                }
                last = dict(work)
                for q in range(4):
                    last[4 * PROJ + SPREAD_ENDS[q]] = square_tiles(next_norm, spread_before + KD * (FFN_TURNS - 1), q)
                last[4 * PROJ] = lambda n: load_root(next_norm)
                stage(n0, FFN_TURNS, FFN_CHUNKS, 0, lambda i: work, last, gates=4)

            ffn(N_FFN1, 0, 1, KD)
            root(1, rs[:, 0, :], rs[:, 2, :])

            for g, (dst, src) in enumerate((
                    (conv_past[:].rearrange("p k c -> p (k c)"), bank[5][:, 0:256]),
                    (pool_past[:, 0:4, :].rearrange("p k c -> p (k c)"), bank[6][:, 0:480]),
                    (pool_past[:, 4:8, :].rearrange("p k c -> p (k c)"), bank[7][:, 0:480]))):
                act.wait_ge(turned, 14 + g)
                act.activation(dst, src, ACT.Copy).then_inc(past_done, 1)

            def place_past(a, g):
                act.wait_ge(rstd_done, 1)
                if a:
                    act.wait_ge(hid_done, 4 * FFN_TURNS + 2 * a)
                for t in range(2):
                    last = act.activation(past_of(zbuf[:, t, META + SEQ:], SEG_Z, POOL_PAST),
                                          pool_past[:, 2 * g + t, :].rearrange("p (s c) -> p s c", s=SEQS), ACT.Copy)
                last.then_inc(z_past, 1)

            def keep_z(a, g):
                for t in range(2):
                    act.wait_ge(z_done, 2 * a + t + 1)
                    act.activation(ztail[:, 2 * g + t, 0:POOL_PAST],
                                   zbuf[:, t, META + SEQ - POOL_PAST:META + SEQ], ACT.Copy)
                    last = act.activation(ztail[:, 2 * g + t, POOL_PAST:].rearrange("p (s c) -> p s c", s=SEQS),
                                          steps_of(zbuf[:, t, META + SEQ:], SEG_Z, POOL_PAST), ACT.Copy)
                last.then_inc(z_kept, 1)

            def split_pooled(j):
                if j in POOL_SPLITS:
                    b = POOL_SPLITS[j]
                    hid_split((2 * (b % 2), 2 * (b % 2) + 1), LIVE, sums[pool_source(b)])

            act.wait_ge(past_done, 3)
            for j, (kind, a) in enumerate(POOL_PLAN):
                if kind == PROJ - 2:
                    place_past(a, POOL_ORDER[a])
                if kind == PROJ - 1:
                    keep_z(a, POOL_ORDER[a])
                if POOL_SPLITS.get(j) == 3:
                    chunk_used(N_POOL + j)
                split_pooled(j)
                split(N_POOL + j + SLOTS)

            def conv_work(i):
                def place_past(tiles):
                    def work(n):
                        for t in tiles:
                            act.activation(
                                past_of(pbuf[:, t, CONV_PAST + SEQ:], SEG_C, CONV_PAST),
                                conv_past[:, bass.ds(i * 4 + t, 1), :].rearrange("p k (s c) -> p (k s) c", s=SEQS),
                                ACT.Copy).then_inc(placed, 1)
                    return work

                def keep_tails(tiles):
                    def work(n):
                        for t in tiles:
                            act.wait_ge(p_done, p.at(1))
                            p.up()
                            act.activation(ctail[:, bass.ds(i * 4 + t, 1), 0:CONV_PAST],
                                           pbuf[:, t:t + 1, SEQ:SEQ + CONV_PAST], ACT.Copy)
                            act.activation(
                                ctail[:, bass.ds(i * 4 + t, 1), CONV_PAST:].rearrange("p k (s c) -> p (k s) c", s=SEQS),
                                steps_of(pbuf[:, t, CONV_PAST + SEQ:], SEG_C, SEG_C - CONV_PAST),
                                ACT.Copy).then_inc(tails_done, 1)
                    return work
                return {
                    PROJ - 1: place_past((0, 1)),
                    2 * PROJ + 1: keep_tails((0, 1)),
                    3 * PROJ - 1: place_past((2, 3)),
                    4 * PROJ + 1: keep_tails((2, 3)),
                    5 * PROJ - 1: lambda n: hid_split((0, 1), LIVE),
                    6 * PROJ - 1: lambda n: hid_split((2, 3), LIVE),
                }
            stage(N_CONV, CONV_TURNS, CONV_CHUNKS, 4, conv_work)

            def sig_and_split(tiles):
                def work(n):
                    sigmoids(tb, tb, tiles, LIVE)(n)
                    hid_split(tiles, LIVE)
                return work

            mix_work = {
                PROJ - 1: sigmoids(ta, ta, (0, 1), LIVE),
                2 * PROJ - 1: sigmoids(ta, ta, (2, 3), LIVE),
                3 * PROJ - 1: sig_and_split((0, 1)),
                4 * PROJ - 1: sig_and_split((2, 3)),
            }
            mix_last = dict(mix_work)
            mix_last[4 * PROJ] = lambda n: load_root(2)
            for q in range(4):
                mix_last[4 * PROJ + SPREAD_ENDS[q]] = square_tiles(2, SPREAD_MIX + KD * MIX_TURNS, q)
            stage(N_MIX, MIX_TURNS, MIX_CHUNKS, 0, lambda i: mix_work, mix_last, gates=8)

            root(2, rs[:, 0, META:T], rs[:, 2, META:T])

            def tail_copy(g):
                act.wait_ge(turned, 16 + g + 1)
                n_rows, dst = (ZTAIL, ztail_rows[:, 512 * g:512 * g + 512]) if g < 2 else (
                    CTAIL, ctail_rows[:, 512 * (g - 2):512 * (g - 2) + 512])
                act.activation(dst, bank[TAIL_BANKS[g]][0:n_rows, :], ACT.Copy).then_inc(tail_rows, 1)
            for g in range(6):
                tail_copy(g)

            ffn(N_FFN2, META, 3, SPREAD_FFN2 + KD)
            root(3, tok[:, 1, :], tok[:, 3, :])
            act.wait_ge(tails_stored, 16 * (4 + SEQS))
            act.wait_ge(rstd_tok, 1)
            for j in range(0, 12, 2):
                kg, t = j // 3, j % 3
                n_rows = Y_ROWS[t][1]
                act.wait_ge(turned, 22 + j + 1)
                act.activation(rows[0:n_rows, t, 512 * kg:512 * kg + 512], bank[j % 7][0:n_rows, :],
                               ACT.Copy, scale=tok[0:n_rows, 4, t:t + 1]).then_inc(rows_act, 1)

        @block.vector
        def _(dve):
            ch = Chunks()
            sig, hh, stp = Tally(sig_done), Tally(hid_hi_done), Tally(step)
            plc, pd, full = Tally(placed), Tally(p_done), Tally(bank_full)
            tallies = (sig, hh, stp, plc, pd, full)

            def split(n):
                if ch.i is None and n >= N_ALL:
                    return
                dve.wait_ge(hi_done, ch.count(n + 1))
                dve.tensor_tensor(w_lo[:, n % SLOTS, :], raw[:, n % RAW, :],
                                  w_hi[:, n % SLOTS, :].bitcast(F32), ALU.subtract).then_inc(lo_done, 1)

            def chunk_used(n):
                dve.wait_ge(used, ch.count(SLOTS + n + 1))

            def stepped(instruction):
                instruction.then_inc(step, 1)
                stp.up()
                dve.wait_ge(step, stp.at())

            def spread_ready(n, m):
                if m < 3:
                    full.up()
                    dve.wait_ge(bank_full, full.at())
                else:
                    chunk_used(n)

            def body(n0, chunks, work):
                for j in range(chunks):
                    if j in work:
                        work[j](n0 + j)
                    split(n0 + j + SLOTS)

            def stage(n0, times, chunks, per, work, last_work=None):
                loops = times if last_work is None else times - 1
                with dve.Fori(0, loops) as i:
                    ch.enter(i, chunks)
                    for x, k in zip(tallies, per):
                        x.enter(i, k)
                    body(n0, chunks, work(i))
                ch.leave()
                for x in tallies:
                    x.leave(loops)
                if last_work is not None:
                    body(n0 + loops * chunks, chunks, last_work)

            def hid_split(tiles, width, src=None):
                for t in tiles:
                    dve.wait_ge(hid_hi_done, hh.at(1))
                    hh.up()
                    x = ta[:, t, 0:width] if src is None else src[:, t % 2, 0:width]
                    dve.tensor_tensor(hid_lo[:, t, 0:width], x, hid_hi[:, t, 0:width].bitcast(F32),
                                      ALU.subtract).then_inc(hid_lo_done, 1)

            def lo_of_tile(norm, gain, k):
                dve.wait_ge(xt_hi, KD * norm + k + 1)
                dve.scalar_tensor_tensor(out=xn_lo[:, k, first_of(norm):T], in0=h[:, k, first_of(norm):T],
                                         scalar=vecs[:, gain + k:gain + k + 1],
                                         in1=xn_hi[:, k, first_of(norm):T].bitcast(F32),
                                         op0=ALU.mult, op1=ALU.subtract).then_inc(xn_done, 1)

            def add_square(norm, k):
                first = first_of(norm)
                dve.wait_ge(sq_done, KD * (norm - 1) + k + 1)
                if k == 0:
                    dve.tensor_copy(ssum[:, first:T], tb[:, 0, first:T]).then_inc(ssum_done, 1)
                else:
                    dve.wait_ge(ssum_done, KD * (norm - 1) + k)
                    dve.tensor_tensor(ssum[:, first:T], ssum[:, first:T], tb[:, k % 4, first:T],
                                      ALU.add).then_inc(ssum_done, 1)

            def mean(x, v):
                return dve.tensor_scalar(v, x, 1.0 / D, EPS, ALU.mult, ALU.add)

            def inverse_root(norm, v, inverse, root, out):
                dve.wait_ge(root_in, norm + 1)
                stepped(dve.reciprocal(inverse, v))
                dve.wait_ge(root_done, norm + 1)
                stepped(dve.tensor_tensor(inverse, root, inverse, ALU.mult))
                stepped(dve.scalar_tensor_tensor(out=root, in0=inverse, scalar=-0.5, in1=root,
                                                 op0=ALU.mult, op1=ALU.mult))
                return dve.scalar_tensor_tensor(out=out, in0=root, scalar=1.5, in1=inverse,
                                                op0=ALU.add, op1=ALU.mult)

            def rms_of_channels(norm, b):
                dve.wait_ge(summed, norm)
                first = first_of(norm)
                mean(bank[b][:, 0:T - first], rs[:, 0, first:T]).then_inc(root_in, 1)
                inverse_root(norm, rs[:, 0, first:T], rs[:, 1, first:T], rs[:, 2, first:T],
                             rstd[:, first:T]).then_inc(rstd_done, 1)
                dve.wait_ge(rstd_done, norm)

            dve.sem_inc(lo_done, RAW)
            dve.sem_inc(spread_done, KD)
            dve.memset(tok[:], 1.0).then_inc(tok_set, 1)
            for j in range(12):
                t, kg = j // 4, j % 4
                first, count = X_ROWS[t]
                if j == 8:
                    dve.wait_ge(turned, 9)
                    dve.tensor_copy(vecs[:], bank[4][:, 0:P]).then_inc(vecs_done, 1)
                dve.wait_ge(turned, j + 1 + (j >= 8))
                dve.tensor_copy(h[:, 4 * kg:4 * kg + 4, first:first + count],
                                bank[j % 8][:, 0:4 * count].rearrange("p (k c) -> p k c", k=4)).then_inc(x_copied, 1)
            dve.wait_ge(vecs_done, 1)
            for n in range(SLOTS):
                split(n)
                for k in range(4 * n, 4 * n + 4):
                    lo_of_tile(0, G_FFN1, k)
                if n == 0:
                    dve.wait_ge(tok_set, 1)
                    dve.wait_ge(tok_sq, 3)
                    mean(tok[:, 0, :], tok[:, 1, :]).then_inc(root_in, 1)
                if n == 1:
                    stepped(inverse_root(0, tok[:, 1, :], tok[:, 2, :], tok[:, 3, :], tok[:, 4, :]))
                    dve.wait_ge(ident_done, 1)
                    for t, (first, count) in enumerate(X_ROWS):
                        dve.tensor_scalar(tb[0:count, t, 0:count], ident[0:count, 0:count],
                                          tok[0:count, 4, t:t + 1], None, ALU.mult).then_inc(diag_done, 1)
            dve.wait_ge(rstd_in, 1)
            stepped(dve.tensor_copy(rstd[:], bank[5][:, 0:T]))

            def ffn(n0, first_token, next_norm):
                width = T - first_token

                def silu(tiles, banks):
                    def work(n):
                        chunk_used(n)
                        for t, b in zip(tiles, banks):
                            dve.tensor_tensor(ta[:, t, 0:width], bank[b][:, 0:width], rstd[:, first_token:T],
                                              ALU.mult).then_inc(gate_done, 1)
                        for t in tiles:
                            dve.wait_ge(sig_done, sig.at(1))
                            sig.up()
                            dve.tensor_tensor(ta[:, t, 0:width], ta[:, t, 0:width], tb[:, t, 0:width],
                                              ALU.mult).then_inc(step, 1)
                            stp.up()
                        for t in tiles:
                            dve.wait_ge(step, stp.at(-1))
                            dve.tensor_tensor(ta[:, t, 0:width], ta[:, t, 0:width], rstd[:, first_token:T],
                                              ALU.mult).then_inc(step, 1)
                            stp.up()
                    return work

                def times_up(tiles, banks):
                    def work(n):
                        chunk_used(n)
                        dve.wait_ge(step, stp.at())
                        for t, b in zip(tiles, banks):
                            dve.tensor_tensor(ta[:, t, 0:width], ta[:, t, 0:width], bank[b][:, 0:width],
                                              ALU.mult).then_inc(hid_done, 1)
                        hid_split(tiles, width)
                    return work

                def add_half(q, norm=None):
                    def work(n):
                        for m in range(4 * q, 4 * q + 4):
                            spread_ready(n, m % 4)
                            out = h[:, m, first_token:T]
                            dve.scalar_tensor_tensor(out=out, in0=bank[m % 8][:, 0:width], scalar=0.5,
                                                     in1=out, op0=ALU.mult, op1=ALU.add).then_inc(spread_done, 1)
                        if norm is not None:
                            for m in range(4 * q, 4 * q + 4):
                                add_square(norm, m)
                                if norm < 3:
                                    lo_of_tile(norm, GAINS[norm], m)
                    return work

                work = {
                    PROJ - 1: silu((0, 1), (0, 1)),
                    2 * PROJ - 1: times_up((0, 1), (2, 3)),
                    3 * PROJ - 1: silu((2, 3), (4, 5)),
                    4 * PROJ - 1: times_up((2, 3), (6, 7)),
                }
                last = dict(work)
                for q in range(4):
                    work[4 * PROJ + SPREAD_ENDS[q]] = add_half(q)
                    last[4 * PROJ + SPREAD_ENDS[q]] = add_half(q, next_norm)
                stage(n0, FFN_TURNS, FFN_CHUNKS, (4, 4, 8, 0, 0, 12), lambda i: work, last)

            ffn(N_FFN1, 0, 1)
            rms_of_channels(1, 4)
            rstd_squared = ssum
            stepped(dve.tensor_tensor(rstd_squared[:], rstd[:], rstd[:], ALU.mult))

            def pool_group(n, a, g):
                window = WINDOWS[g]
                dve.wait_ge(hid_lo_done, 4 * FFN_TURNS + 2 * a)
                if a:
                    dve.wait_ge(z_kept, a)
                chunk_used(n)
                for t in range(2):
                    zt = bank[Z_BANKS[a][t]]
                    dve.tensor_tensor(zbuf[:, t, 0:META + SEQ], zt[:, 0:META + SEQ], rstd[:, 0:META + SEQ], ALU.mult)
                    dve.tensor_tensor(steps_of(zbuf[:, t, META + SEQ:], SEG_Z, POOL_PAST),
                                      zt[:, META + SEQ:T].rearrange("p (s c) -> p s c", s=SEQS),
                                      rstd[:, META + SEQ:T].rearrange("p (s c) -> p s c", s=SEQS),
                                      ALU.mult).then_inc(z_done, 1)
                dve.wait_ge(z_past, a + 1)
                for t in range(2):
                    dve.wait_ge(z_done, 2 * a + t + 1)
                    src, d, w = zbuf[:, t, :], 1, 0
                    while d < window:
                        dst = sums[w][:, t, :]
                        stepped(dve.tensor_tensor(dst[:, 2 * d - 1:ZBUF], src[:, 2 * d - 1:ZBUF],
                                                  src[:, d - 1:ZBUF - d], ALU.add))
                        src, d, w = dst, 2 * d, 1 - w
                    z, out = zbuf[:, t, :], sums[w][:, t, :]
                    dve.scalar_tensor_tensor(out=out[:, 0:SEQ], in0=src[:, META:META + SEQ], scalar=1.0 / window,
                                             in1=z[:, META:META + SEQ], op0=ALU.mult, op1=ALU.subtract)
                    dve.scalar_tensor_tensor(
                        out=out[:, SEQ:LIVE].rearrange("p (s c) -> p s c", s=SEQS),
                        in0=steps_of(src[:, META + SEQ:], SEG_Z, POOL_PAST), scalar=1.0 / window,
                        in1=steps_of(z[:, META + SEQ:], SEG_Z, POOL_PAST), op0=ALU.mult,
                        op1=ALU.subtract).then_inc(hid_done, 1)

            def split_pooled(j):
                if j in POOL_SPLITS:
                    b = POOL_SPLITS[j]
                    hid_split((2 * (b % 2), 2 * (b % 2) + 1), LIVE, sums[pool_source(b)])

            for j, (kind, a) in enumerate(POOL_PLAN):
                if kind == PROJ - 1:
                    pool_group(N_POOL + j, a, POOL_ORDER[a])
                if POOL_SPLITS.get(j) != 3:
                    split_pooled(j)
                if kind == "map":
                    for m in range(4):
                        spread_ready(N_POOL + j, m)
                        tile = 4 * POOL_ORDER[a] + m
                        dve.tensor_scalar(ypool[:, tile, :], bank[MAP_BANKS[a][m]][:, 0:LIVE],
                                          vecs[:, G_SCALE + tile:G_SCALE + tile + 1], None,
                                          ALU.mult).then_inc(spread_done, 1)
                if POOL_SPLITS.get(j) == 3:
                    split_pooled(j)
                split(N_POOL + j + SLOTS)

            def spread_into(dst, first, q, norm=None):
                def work(n):
                    for m in range(4 * q, 4 * q + 4):
                        spread_ready(n, m % 4)
                        out = dst[:, m, first:first + LIVE]
                        dve.tensor_tensor(out, out, bank[m % 8][:, 0:LIVE], ALU.add).then_inc(spread_done, 1)
                    if norm is not None:
                        for m in range(4 * q, 4 * q + 4):
                            add_square(norm, m)
                            lo_of_tile(norm, GAINS[norm], m)
                return work

            dve.wait_ge(yconv_zero, 1)

            def conv_work(i):
                def place_v(tiles, banks):
                    def work(n):
                        chunk_used(n)
                        for t, b in zip(tiles, banks):
                            dve.tensor_tensor(tb[:, t, 0:CV], bank[b][:, 0:CV], rstd_squared[:, META - CONV_PAST:T],
                                              ALU.mult).then_inc(step, 1)
                            stp.up()
                    return work

                def convolve(tiles, banks):
                    def work(n):
                        chunk_used(n)
                        dve.wait_ge(step, stp.at())
                        for t, b in zip(tiles, banks):
                            dve.tensor_tensor(pbuf[:, t, 0:CONV_PAST + SEQ], tb[:, t, 0:CONV_PAST + SEQ],
                                              bank[b][:, 0:CONV_PAST + SEQ], ALU.mult)
                            dve.tensor_tensor(
                                steps_of(pbuf[:, t, CONV_PAST + SEQ:], SEG_C, CONV_PAST),
                                tb[:, t, CONV_PAST + SEQ:CV].rearrange("p (s c) -> p s c", s=SEQS),
                                bank[b][:, CONV_PAST + SEQ:CV].rearrange("p (s c) -> p s c", s=SEQS),
                                ALU.mult).then_inc(p_done, 1)
                        width = PBUF - CONV_PAST
                        for t in tiles:
                            pd.up()
                            plc.up()
                            dve.wait_ge(p_done, pd.at())
                            dve.wait_ge(placed, plc.at())

                            def tap(w, t=t):
                                return vecs[:, bass.ds(i * 4 + (G_CONV + 16 * w + t), 1)]
                            stepped(dve.tensor_scalar(tb[:, t, 0:width], pbuf[:, t, 0:width], tap(0), None, ALU.mult))
                            for w in (1, 2):
                                stepped(dve.scalar_tensor_tensor(
                                    out=tb[:, t, 0:width], in0=pbuf[:, t, w:w + width], scalar=tap(w),
                                    in1=tb[:, t, 0:width], op0=ALU.mult, op1=ALU.add))
                    return work

                def times_b(tiles, banks):
                    def work(n):
                        chunk_used(n)
                        for t, b in zip(tiles, banks):
                            dve.tensor_tensor(ta[:, t, 0:LIVE], bank[b][:, 0:LIVE], rstd[:, META:T],
                                              ALU.mult).then_inc(step, 1)
                            stp.up()
                        for t in tiles:
                            dve.wait_ge(step, stp.at(t - tiles[-1]))
                            dve.tensor_tensor(ta[:, t, 0:SEQ], ta[:, t, 0:SEQ], tb[:, t, 0:SEQ], ALU.mult)
                            y = steps_of(tb[:, t, SEQ:SEQ + SEQS * SEG_C], SEG_C, CONV_PAST)
                            b_steps = ta[:, t, SEQ:LIVE].rearrange("p (s c) -> p s c", s=SEQS)
                            dve.tensor_tensor(b_steps, b_steps, y, ALU.mult).then_inc(hid_done, 1)
                        hid_split(tiles, LIVE)
                    return work

                work = {
                    PROJ - 1: place_v((0, 1), (0, 1)),
                    2 * PROJ - 1: convolve((0, 1), (2, 3)),
                    3 * PROJ - 1: place_v((2, 3), (4, 5)),
                    4 * PROJ - 1: convolve((2, 3), (6, 7)),
                    5 * PROJ - 1: times_b((0, 1), (0, 1)),
                    6 * PROJ - 1: times_b((2, 3), (4, 5)),
                }
                for q in range(4):
                    work[6 * PROJ + SPREAD_ENDS[q]] = spread_into(yconv, 0, q)
                return work
            stage(N_CONV, CONV_TURNS, CONV_CHUNKS, (0, 4, 20, 4, 4, 12), conv_work)

            def mix_work(i, norm=None):
                def scale_gates(dst, tiles, banks):
                    for t, b in zip(tiles, banks):
                        dve.tensor_tensor(dst[:, t, 0:LIVE], bank[b][:, 0:LIVE], rstd[:, META:T],
                                          ALU.mult).then_inc(gate_done, 1)

                def gate_conv(tiles, banks):
                    def work(n):
                        chunk_used(n)
                        scale_gates(ta, tiles, banks)
                        for t in tiles:
                            dve.wait_ge(sig_done, sig.at(1))
                            sig.up()
                            dve.tensor_tensor(ta[:, t:t + 1, 0:LIVE], ta[:, t:t + 1, 0:LIVE],
                                              yconv[:, bass.ds(i * 4 + t, 1), :], ALU.mult).then_inc(step, 1)
                            stp.up()
                    return work

                def gate_pool(tiles, banks):
                    def work(n):
                        chunk_used(n)
                        scale_gates(tb, tiles, banks)
                        for t in tiles:
                            dve.wait_ge(sig_done, sig.at(1))
                            sig.up()
                            stepped(dve.tensor_tensor(tb[:, t:t + 1, 0:LIVE], tb[:, t:t + 1, 0:LIVE],
                                                      ypool[:, bass.ds(i * 4 + t, 1), :], ALU.mult))
                            dve.tensor_tensor(ta[:, t, 0:LIVE], ta[:, t, 0:LIVE], tb[:, t, 0:LIVE],
                                              ALU.add).then_inc(hid_done, 1)
                        hid_split(tiles, LIVE)
                    return work

                work = {
                    PROJ - 1: gate_conv((0, 1), (0, 1)),
                    2 * PROJ - 1: gate_conv((2, 3), (2, 3)),
                    3 * PROJ - 1: gate_pool((0, 1), (4, 5)),
                    4 * PROJ - 1: gate_pool((2, 3), (6, 7)),
                }
                for q in range(4):
                    work[4 * PROJ + SPREAD_ENDS[q]] = spread_into(h, META, q, norm)
                return work
            stage(N_MIX, MIX_TURNS, MIX_CHUNKS, (8, 4, 8, 0, 0, 12), mix_work, mix_work(MIX_TURNS - 1, 2))

            rms_of_channels(2, 4)
            ffn(N_FFN2, META, 3)

            dve.wait_ge(summed, 3)
            dve.tensor_scalar(tok[:, 1, 0:2], bank[7][:, 0:4].rearrange("p (t c) -> p t c", c=2)[:, :, 0],
                              1.0 / D, EPS, ALU.mult, ALU.add)
            mean(bank[7][0:SAMP, 4:5], tok[0:SAMP, 1, 2:3]).then_inc(root_in, 1)
            inverse_root(3, tok[:, 1, :], tok[:, 2, :], tok[:, 3, :], tok[:, 4, :]).then_inc(rstd_tok, 1)
            dve.wait_ge(tails_stored, 16 * (4 + SEQS))
            dve.wait_ge(rstd_tok, 1)
            for j in range(1, 12, 2):
                kg, t = j // 3, j % 3
                n_rows = Y_ROWS[t][1]
                dve.wait_ge(turned, 22 + j + 1)
                dve.tensor_scalar(rows[0:n_rows, t, 512 * kg:512 * kg + 512], bank[j % 7][0:n_rows, :],
                                  tok[0:n_rows, 4, t:t + 1], None, ALU.mult).then_inc(rows_dve, 1)


_INS = ['x_prompt', 'x_sample', 'state_conv', 'state_pool', 'meta_tokens', 'norm_ffn1', 'w_ffn1_gate',
        'w_ffn1_up', 'w_ffn1_down', 'norm_mix', 'w_in', 'conv_w', 'w_conv_out', 'w_pool_group',
        'pool_scale', 'w_o', 'norm_ffn2', 'w_ffn2_gate', 'w_ffn2_up', 'w_ffn2_down', 'norm_final']
_OUTS = [(1, SEQ, D), (SEQS, STEPS, D), (1, 1, CONV_PAST, D), (1, 1, POOL_PAST, D // 2),
         (1, SEQS, CONV_PAST, D), (1, SEQS, POOL_PAST, D // 2)]


def kernel(**inputs):
    import numpy as np
    import concourse.bacc as bacc
    from concourse.bass_utils import run_bass_kernel_spmd

    nc = bacc.Bacc("TRN2", target_bir_lowering=False, num_devices=1)
    arrays, args = {}, []
    for name in _INS:
        a = np.ascontiguousarray(inputs[name])
        arrays[f"in_{name}"] = a
        args.append(nc.dram_tensor(f"in_{name}", a.shape, mybir.dt.from_np(a.dtype), kind="ExternalInput").ap())
    for i, shape in enumerate(_OUTS):
        args.append(nc.dram_tensor(f"out_{i}", shape, F32, kind="ExternalOutput").ap())
    build(nc, *args)
    r = run_bass_kernel_spmd(nc, [arrays], core_ids=[0])
    return tuple(r.results[0][f"out_{i}"] for i in range(len(_OUTS)))
```
